# Optimizing a Trainium2 kernel written in Bass

```python
import jax, jax.numpy as jnp
from jax import lax
import numpy as np

D_MODEL = 1024
BATCH = 1
SEQ = 1024
DEPTH = 1

D_MIX = D_MODEL
D_CONV = D_MIX // 2
N_CONV_HEADS = 8
CONV_WIDTH = 31
D_POOL = D_MIX - D_CONV
POOL_WINDOWS = (2, 4, 8, 16)
N_POOL_GROUPS = len(POOL_WINDOWS)
POOL_GROUP_DIM = D_POOL // N_POOL_GROUPS
D_IN = 2 * D_CONV + D_POOL
D_FF = 2816
FFN_CONV_WIDTH = 3
EPS = 1e-6

kernel_name = "hybrid_conformer_pool_convffn_block"

def _rmsnorm(x, g):
    xf = x.astype(jnp.float32)
    y = xf * lax.rsqrt(jnp.mean(xf * xf, axis=-1, keepdims=True) + EPS)
    return (y * g.astype(jnp.float32)).astype(x.dtype)

def _layernorm(x, g, b):
    xf = x.astype(jnp.float32)
    mu = jnp.mean(xf, axis=-1, keepdims=True)
    xc = xf - mu
    var = jnp.mean(xc * xc, axis=-1, keepdims=True)
    y = xc * lax.rsqrt(var + EPS) * g.astype(jnp.float32) + b.astype(jnp.float32)
    return y.astype(x.dtype)

def _causal_dwconv(x, w, b):
    k, c = w.shape
    y = lax.conv_general_dilated(
        x, w[:, None, :].astype(x.dtype), window_strides=(1,),
        padding=((k - 1, 0),), dimension_numbers=("NWC", "WIO", "NWC"),
        feature_group_count=c)
    return y + b

def _conformer_conv_mixer(a_val, a_gate, conv_w, conv_b, ln_g, ln_b):
    h = a_val * jax.nn.sigmoid(a_gate)
    h = _causal_dwconv(h, conv_w, conv_b)
    h = _layernorm(h, ln_g, ln_b)
    return jax.nn.silu(h)

def _multiscale_pool_mixer(xb, pool_w, pool_scale):
    bsz, s, _ = xb.shape
    xg = xb.reshape(bsz, s, N_POOL_GROUPS, POOL_GROUP_DIM).astype(jnp.float32)
    cs = jnp.cumsum(xg, axis=1)
    pos = jnp.arange(1, s + 1, dtype=jnp.float32)
    outs = []
    for gi, w in enumerate(POOL_WINDOWS):
        c = cs[:, :, gi]
        lag = jnp.pad(c[:, : s - w], ((0, 0), (w, 0), (0, 0)))
        cnt = jnp.minimum(pos, float(w))[None, :, None]
        outs.append((c - lag) / cnt - xg[:, :, gi])
    d = jnp.stack(outs, axis=2).astype(xb.dtype)
    y = jnp.einsum("bsgc,gcd->bsgd", d, pool_w).reshape(bsz, s, D_POOL)
    return y * pool_scale

def setup_inputs(seed: int = 0) -> dict:
    key = jax.random.key(seed)
    ks = jax.random.split(key, 17)
    f32 = jnp.float32
    L = DEPTH

    def nrm(k, shape, scale):
        return jax.random.normal(k, shape, f32) * scale

    return {
        "x": jax.random.normal(ks[0], (BATCH, SEQ, D_MODEL), f32),
        "norm_mix_g": 1.0 + nrm(ks[1], (L, D_MODEL), 0.05),
        "w_in": nrm(ks[2], (L, D_MODEL, D_IN), D_MODEL ** -0.5),
        "conv_a_w": nrm(ks[3], (L, CONV_WIDTH, D_CONV), CONV_WIDTH ** -0.5),
        "conv_a_b": nrm(ks[4], (L, D_CONV), 0.02),
        "ln_a_g": 1.0 + nrm(ks[5], (L, D_CONV), 0.05),
        "ln_a_b": nrm(ks[6], (L, D_CONV), 0.02),
        "pool_w": nrm(ks[7], (L, N_POOL_GROUPS, POOL_GROUP_DIM, POOL_GROUP_DIM), POOL_GROUP_DIM ** -0.5),
        "pool_scale": 1.0 + nrm(ks[8], (L, D_POOL), 0.1),
        "w_out": nrm(ks[9], (L, D_MIX, D_MODEL), D_MIX ** -0.5),
        "norm_ffn_g": 1.0 + nrm(ks[10], (L, D_MODEL), 0.05),
        "w_up": nrm(ks[11], (L, D_MODEL, 2 * D_FF), D_MODEL ** -0.5),
        "conv_f_w": nrm(ks[12], (L, FFN_CONV_WIDTH, D_FF), FFN_CONV_WIDTH ** -0.5),
        "conv_f_b": nrm(ks[13], (L, D_FF), 0.02),
        "w_down": nrm(ks[14], (L, D_FF, D_MODEL), D_FF ** -0.5),
        "norm_final_g": 1.0 + nrm(ks[15], (D_MODEL,), 0.05),
    }

def reference(x, norm_mix_g, w_in, conv_a_w, conv_a_b, ln_a_g, ln_a_b, pool_w,
              pool_scale, w_out, norm_ffn_g, w_up, conv_f_w, conv_f_b, w_down,
              norm_final_g):
    for l in range(DEPTH):
        h = _rmsnorm(x, norm_mix_g[l])
        proj = h @ w_in[l]
        a_val, a_gate, b_in = jnp.split(proj, [D_CONV, 2 * D_CONV], axis=-1)
        ya = _conformer_conv_mixer(a_val, a_gate, conv_a_w[l], conv_a_b[l],
                                   ln_a_g[l], ln_a_b[l])
        yb = _multiscale_pool_mixer(b_in, pool_w[l], pool_scale[l])
        x = x + jnp.concatenate([ya, yb], axis=-1) @ w_out[l]
        h = _rmsnorm(x, norm_ffn_g[l])
        gate, val = jnp.split(h @ w_up[l], 2, axis=-1)
        gate = _causal_dwconv(gate, conv_f_w[l], conv_f_b[l])
        x = x + (jax.nn.silu(gate) * val) @ w_down[l]
    return _rmsnorm(x, norm_final_g)


_drawn_inputs = setup_inputs


def setup_inputs(seed=0):
    import zlib

    import numpy as np

    out = dict(_drawn_inputs(seed))
    spreads = {}
    factors = {'conv_a_b': 3.925, 'ln_a_b': 7.258, 'conv_f_b': 6.64}
    for name, (base, spread) in spreads.items():
        noise = np.random.default_rng([zlib.crc32(name.encode()), seed]).standard_normal(out[name].shape)
        drawn = base * np.exp(spread * noise) if base else spread * noise
        out[name] = __import__('jax').numpy.asarray(drawn.astype(out[name].dtype))
    for name, factor in factors.items():
        out[name] = (out[name] * factor).astype(out[name].dtype)
    return out
```

```python
from contextlib import ExitStack

import concourse.bass as bass
from concourse import mybir

P = 128
BANK = 512
F32 = mybir.dt.float32
F32R = mybir.dt.float32r
ALU = mybir.AluOpType
ACT = mybir.ActivationFunctionType


def hybrid_block(nc, x, norm_mix_g, w_in, conv_a_w, conv_a_b, ln_a_g, ln_a_b, pool_w, pool_scale,
                 w_out, norm_ffn_g, w_up, conv_f_w, conv_f_b, w_down, norm_final_g, out):
    _, SEQ, D = x.shape
    DEPTH, TAPS, D_CONV = conv_a_w.shape
    GROUPS, GDIM = pool_w.shape[1:3]
    D_FF = w_down.shape[1]
    FTAPS = conv_f_w.shape[1]
    WINDOWS = (2, 4, 8, 16)
    EPS = 1e-6
    KT = D // P
    TT = SEQ // P
    HALF = SEQ // 2
    HT = TT // 2
    CT = D_CONV // P
    FT = D_FF // P
    CHUNKS = FT // 2
    W2 = 2 * P
    assert DEPTH == 1 and SEQ == D == 2 * BANK and GDIM == P and GROUPS == CT == 4
    assert FT == 2 * CHUNKS and CHUNKS % 2 == 1 and FTAPS == 3 and KT == TT == 8

    x_rows = x.rearrange("b (m p) d -> p (b m) d", p=P)
    out_rows = out.rearrange("b (m p) d -> p (b m) d", p=P)
    w_in_v = w_in[0].rearrange("(k p) n -> p k n", p=P)
    w_out_v = w_out[0].rearrange("(k p) n -> p k n", p=P)
    w_up_v = w_up[0].rearrange("(k p) n -> p k n", p=P)
    w_down_v = w_down[0].rearrange("(k p) n -> p k n", p=P)
    pool_w_v = pool_w[0].rearrange("g c d -> c g d")

    counter = [0]

    def jobs(n):
        counter[0] += n
        return list(range(counter[0] - n, counter[0]))

    J_CONST = jobs(1)[0]
    J_T1 = jobs(TT)
    J_IN = jobs(2 * CT + GROUPS)
    J_LN, J_BACK = [jobs(2)], []
    J_POOL = jobs(GROUPS)
    J_BACK.append(jobs(2))
    J_OUT, J_T2 = [], []
    for m in range(TT):
        if m == HT:
            J_LN.append(jobs(2))
            J_BACK.append(jobs(2))
        J_OUT += jobs(1)
        if m % HT:
            J_T2 += jobs(1)
        if m % HT == HT - 1:
            J_T2 += jobs(1)
    UPS = 4
    J_FFN = jobs(UPS)[0]
    J_BODY = counter[0]
    BODY = UPS + TT

    def up_job(i, r):
        return J_FFN + r if isinstance(i, int) and i == 0 else i * BODY + (J_BODY - BODY + r)

    def down_job(i, m):
        if isinstance(i, int) and i == CHUNKS - 1:
            return J_BODY + i * BODY + m
        return i * BODY + (J_BODY + UPS + m)

    IN_COLS = (0, D_CONV, W2, D_CONV + W2, 2 * D_CONV + W2, 2 * D_CONV)
    OUT_ROWS = (4, 6, 0, 2)
    U_OUT = len(IN_COLS)
    U_FFN = U_OUT + len(OUT_ROWS)
    W_SLOT = (0, 1, 2, 0, 1, 2, 0, 1, 2, 3)
    FFN_SLOT = {"g": 0, "v": 1, "d": 2}
    DVE_UNITS = 2
    HI0, LO0 = 2 * U_FFN, 2 * DVE_UNITS

    def ffn_half(kind, i, t):
        if kind == "d":
            return 6 * (CHUNKS - 1) + 5 + t if isinstance(i, int) and i == CHUNKS - 1 else i * 6 + (9 + t)
        o = 2 * t + (kind == "v")
        return 1 + o if isinstance(i, int) and i == 0 else i * 6 + (o - 1)

    def raw_loads(q, par):
        return q * 8 + (16 - 8 * par)

    with ExitStack() as ctx:
        def sb(name, shape, dt=F32):
            return ctx.enter_context(nc.sbuf_tensor(name, shape, dt))

        def sem(name):
            return ctx.enter_context(nc.semaphore(name))

        ROWS = TAPS + 4
        BIAS, LN_G, LN_B, SCALE = range(TAPS, ROWS)
        x_sb = sb("x_sb", [P, TT, D])
        act_hi = sb("act_hi", [P, KT, SEQ], F32R)
        act_lo = sb("act_lo", [P, KT, SEQ], F32R)
        raw = sb("raw", [P, 2, 2 * D])
        w_hi = [sb(f"w_hi{s}", [P, 2 * D], F32R) for s in range(3)]
        w_lo = [sb(f"w_lo{s}", [P, 2 * D], F32R) for s in range(3)]
        tmp = sb("tmp", [P, 2, SEQ])
        ident = sb("ident", [P, P])
        chan = sb("chan", [P, CT, ROWS])
        fchan = sb("fchan", [P, FT, FTAPS + 1])
        inv_count = sb("inv_count", [P, WINDOWS[-1]])
        edge = sb("edge", [P, WINDOWS[-1]])
        eps = sb("eps", [P, 1])
        IN, FFN, FINAL, LN = range(4)
        sumsq = sb("sumsq", [P, 3, TT])
        std = sb("std", [P, 4, TT])
        rstd = sb("rstd", [P, 4, TT])
        bn = sb("bn", [P, TT, 6])
        mean_var = sb("mean_var", [P, TT, 2])
        shift = sb("shift", [P, TT])
        with nc.sbuf_tensor("pw_hi", [P, GROUPS, P], F32R) as pw_hi:
            with nc.sbuf_tensor("pw_lo", [P, GROUPS, P], F32R) as pw_lo:
                pass
        gain = sb("gain", [P, D])
        with nc.sbuf_tensor("conv", [P, 2, CT, HALF], F32) as conv:
            with nc.sbuf_tensor("tokens", [P, GROUPS, SEQ], F32) as tokens:
                pass
            with nc.sbuf_tensor("w_hi3", [P, 2 * D], F32R) as w_hi3:
                with nc.sbuf_tensor("w_lo3", [P, 2 * D], F32R) as w_lo3:
                    pass
        gv_hi = sb("gv_hi", [P, 2, 2, SEQ], F32R)
        gv_lo = sb("gv_lo", [P, 2, 2, SEQ], F32R)
        w_hi.append(w_hi3)
        w_lo.append(w_lo3)
        raw_rows = conv[:, 0, 0, :]
        raw_frows = tokens[:, :, :].rearrange("p a b -> p (a b)")[:, 0:D_FF]
        pw_raw = conv[:, 1, 0, :].rearrange("p (g d) -> p g d", g=GROUPS)
        u = x_sb[:, HT:TT, :]

        slot = [ctx.enter_context(nc.psum_tensor(f"slot{s}", [P, 2 * BANK], F32)) for s in range(4)]

        def slot_of(n):
            return slot[n % 4]

        consts_loaded = sem("consts_loaded")
        pool_w_loaded = sem("pool_w_loaded")
        gain_loaded = sem("gain_loaded")
        x_loaded = [sem(f"x_loaded{m}") for m in range(TT)]
        raw_loaded = [sem(f"raw_loaded{b}") for b in range(2)]
        stored = [sem(f"stored{b}") for b in range(4)]
        ident_ready = sem("ident_ready")
        small_ready = sem("small_ready")
        pe_done = sem("pe_done")
        chan_ready = sem("chan_ready")
        hi_done = sem("hi_done")
        lo_done = sem("lo_done")
        lo_pool_done = sem("lo_pool_done")
        pw_done = sem("pw_done")
        squares_done = sem("squares_done")
        std_done = sem("std_done")
        rstd_done = sem("rstd_done")
        normed = sem("normed")
        act_hi_done = sem("act_hi_done")
        act_lo_done = sem("act_lo_done")
        sig_done = sem("sig_done")
        u_done = sem("u_done")
        conv_step = sem("conv_step")
        tokens_ready = sem("tokens_ready")
        window_step = sem("window_step")
        d_step = sem("d_step")
        ln_step = sem("ln_step")
        ln_std_done = sem("ln_std_done")
        z_done = sem("z_done")
        silu_done = sem("silu_done")
        x1_done = sem("x1_done")
        last_tap_done = sem("last_tap_done")
        gate_one = sem("gate_one")
        gate_taps = sem("gate_taps")
        gate_silu = sem("gate_silu")
        gated = sem("gated")
        gv_hi_done = sem("gv_hi_done")
        gv_lo_done = sem("gv_lo_done")
        x_added = sem("x_added")
        x2_done = sem("x2_done")
        out_ready = sem("out_ready")

        T1_DONE = 0
        DIFF_DONE = T1_DONE + TT
        YB_DONE = DIFF_DONE + GROUPS
        YA_DONE = [YB_DONE + GROUPS, YB_DONE + GROUPS + CT + HT]
        T2_DONE = [YA_DONE[0] + CT, YA_DONE[1] + CT]

        WINDOW_STEPS = [sum(2 * (k + 1) for k in range(g, GROUPS)) for g in range(GROUPS)]
        LN_STEPS = 2 * HT + 2

        read = {J_CONST: (chan_ready, 2)}
        read |= {J_T1[m]: (act_lo_done, T1_DONE + m + 1) for m in range(TT)}
        for j in range(CT):
            read[J_IN[2 * j]] = (u_done, j + 1)
            read[J_IN[2 * j + 1]] = (sig_done, j + 1)
            read[J_IN[2 * CT + j]] = (tokens_ready, j + 1)
            read[J_POOL[j]] = (act_lo_done, YB_DONE + j + 1)
        for h in range(2):
            for b in range(2):
                read[J_LN[h][b]] = (z_done, HT * h + 2 * b + 2)
                read[J_BACK[h][b]] = (act_lo_done, YA_DONE[h] + 2 * b + 2)
        for m in range(TT):
            read[J_OUT[m]] = (x1_done, m + 1)
            read[J_T2[m]] = (act_lo_done, T2_DONE[m // HT] + m % HT + 1)

        def half_of(buf, columns, t):
            if columns:
                return buf.rearrange("p (k n) -> p k n", k=KT)[:, :, t * P:(t + 1) * P]
            return buf[:, t * D:(t + 1) * D]

        def whole(buf, columns):
            return buf.rearrange("p (k n) -> p k n", k=KT if columns else 2)

        block = ctx.enter_context(nc.Block())

        @block.sync
        def _(sp):
            def load_x(m):
                sp.dma_start(x_sb[:, m, :], x_rows[:, m, :]).then_inc(x_loaded[m], 16)

            def load_gain(src):
                sp.dma_start(gain[:, :], src.broadcast_to([P, D])).then_inc(gain_loaded, 16)

            def load_unit(q):
                if q >= 2 + DVE_UNITS:
                    sp.wait_ge(lo_pool_done, 2 * (q - 2 - DVE_UNITS) + 2)
                elif q >= 2:
                    sp.wait_ge(lo_done, 2 * (q - 2) + 2)
                if q < U_OUT:
                    src = w_in_v[:, :, IN_COLS[q]:IN_COLS[q] + W2]
                else:
                    src = w_out_v[:, OUT_ROWS[q - U_OUT]:OUT_ROWS[q - U_OUT] + 2, :]
                sp.dma_start(whole(raw[:, q % 2, :], q < U_OUT), src).then_inc(raw_loaded[q % 2], 16)

            def load_ffn(kind, i, par):
                if kind == "d":
                    src = w_down_v[:, bass.ds(i * 2, 2), :]
                else:
                    src = w_up_v[:, :, bass.ds(i * W2 + (D_FF if kind == "v" else 0), W2)]
                sp.dma_start(whole(raw[:, par, :], kind != "d"), src).then_inc(raw_loaded[par], 16)

            load_x(0)
            load_gain(norm_mix_g)
            load_x(1)
            load_x(2)
            load_unit(0)
            load_x(3)
            load_unit(1)
            for m in range(HT, TT):
                load_x(m)
            for q in range(2, U_FFN):
                load_unit(q)
            sp.wait_ge(pe_done, J_POOL[-1] + 1)
            load_gain(norm_ffn_g)
            sp.wait_ge(lo_pool_done, 2 * (U_FFN - DVE_UNITS) - 2)
            load_ffn("g", 0, 0)
            sp.wait_ge(lo_pool_done, 2 * (U_FFN - DVE_UNITS))
            load_ffn("v", 0, 1)
            for j in range(CT):
                sp.wait_ge(conv_step, TAPS * (CT + j + 1))
                load_x(HT + j)
            sp.wait_ge(lo_done, LO0 + ffn_half("g", 0, 1))
            load_ffn("g", 1, 0)
            sp.wait_ge(lo_done, LO0 + ffn_half("v", 0, 1))
            load_ffn("v", 1, 1)

            def body(i, par, last=False):
                sp.wait_ge(lo_done, ffn_half("g", i, 1) + LO0)
                load_ffn("d", i - 1, par)
                if not last:
                    sp.wait_ge(lo_done, ffn_half("v", i, 1) + LO0)
                    load_ffn("g", i + 1, 1 - par)
                    sp.wait_ge(lo_done, ffn_half("d", i - 1, 1) + LO0)
                    load_ffn("v", i + 1, par)

            with sp.Fori(1, CHUNKS - 2, 2) as i:
                body(i, 0)
                body(i + 1, 1)
            body(CHUNKS - 2, 0)
            body(CHUNKS - 1, 1, last=True)
            sp.wait_ge(lo_done, LO0 + ffn_half("v", CHUNKS - 1, 1))
            load_ffn("d", CHUNKS - 1, 0)
            sp.wait_ge(normed, 2 * TT)
            load_gain(norm_final_g.rearrange("(a d) -> a d", a=1))
            for m in range(TT):
                sp.wait_ge(out_ready, m + 1)
                sp.dma_start(out_rows[:, m, :], raw[:, m % 4 // 2, (m % 2) * D:(m % 2 + 1) * D])\
                  .then_inc(stored[m % 4], 16)
            for b in range(4):
                sp.wait_ge(stored[b], 16 * TT // 4)

        @block.gpsimd
        def _(pool):
            nc.gpsimd.memset(ident[:, :], 0.0).then_inc(ident_ready, 1)
            pool.wait_ge(ident_ready, 1)
            nc.gpsimd.affine_select(out=ident[:, :], in_=ident[:, :], compare_op=ALU.not_equal, fill=1.0,
                                    base=0, pattern=[[-1, P]], channel_multiplier=1).then_inc(ident_ready, 1)
            nc.gpsimd.memset(eps[:, :], EPS).then_inc(small_ready, 1)
            for t in range(WINDOWS[-1]):
                nc.gpsimd.memset(inv_count[:, t:t + 1], 1.0 / (t + 1)).then_inc(small_ready, 1)

            def unit_lo(q):
                s, columns = W_SLOT[q], q < U_OUT
                for t in range(2):
                    pool.wait_ge(hi_done, 2 * q + t + 1)
                    nc.gpsimd.tensor_tensor(half_of(w_lo[s][:, :], columns, t),
                                            half_of(raw[:, q % 2, :], columns, t),
                                            half_of(w_hi[s][:, :].bitcast(F32), columns, t),
                                            ALU.subtract).then_inc(lo_pool_done, 1)

            def windows(g, before):
                pool.wait_ge(tokens_ready, GROUPS - g)
                if g == GROUPS - 1:
                    pool.wait_ge(u_done, CT)
                else:
                    pool.wait_ge(d_step, 3 * (GROUPS - 1 - g))
                src = tokens[:, g, :]
                for b in range(g + 1):
                    w, dst = 2 ** b, tmp[:, b % 2, :]
                    if b:
                        pool.wait_ge(window_step, before + 2 * b)
                    nc.gpsimd.tensor_tensor(dst[:, w:SEQ], src[:, w:SEQ], src[:, 0:SEQ - w],
                                            ALU.add).then_inc(window_step, 1)
                    nc.gpsimd.tensor_copy(dst[:, 0:w], src[:, 0:w]).then_inc(window_step, 1)
                    src = dst

            for q in range(DVE_UNITS, 7):
                unit_lo(q)
            windows(3, 0)
            unit_lo(7)
            windows(2, WINDOW_STEPS[3])
            windows(1, WINDOW_STEPS[2])
            windows(0, WINDOW_STEPS[1])
            unit_lo(8)
            unit_lo(9)

        @block.scalar
        def _(act):
            act.dma_start(raw_rows[0:TAPS, :], conv_a_w[0]).then_inc(consts_loaded, 16)
            for r, v in ((BIAS, conv_a_b), (LN_G, ln_a_g), (LN_B, ln_a_b), (SCALE, pool_scale)):
                act.dma_start(raw_rows[r:r + 1, :], v).then_inc(consts_loaded, 16)
            act.dma_start(raw_frows[0:FTAPS, :], conv_f_w[0]).then_inc(consts_loaded, 16)
            act.dma_start(raw_frows[FTAPS:FTAPS + 1, :], conv_f_b).then_inc(consts_loaded, 16)
            act.dma_start(pw_raw, pool_w_v).then_inc(pool_w_loaded, 16)

            def norm_std(row, m):
                n = row * TT + m + 1
                act.wait_ge(squares_done, n - 1)
                nc.scalar.activation(tmp[:, m % 2, :], x_sb[:, m, :], ACT.Square,
                                     accum_out=sumsq[:, row, m:m + 1]).then_inc(squares_done, 1)
                act.wait_ge(squares_done, n)
                nc.scalar.activation(std[:, row, m:m + 1], sumsq[:, row, m:m + 1], ACT.Sqrt,
                                     bias=eps[:, 0:1], scale=1.0 / D).then_inc(std_done, 1)

            def transposed_hi(n, m):
                act.wait_ge(pe_done, n + 1)
                nc.scalar.activation(act_hi[:, :, m * P:(m + 1) * P],
                                     slot_of(n)[:, :].rearrange("p (k n) -> p k n", k=KT),
                                     ACT.Copy).then_inc(act_hi_done, 1)

            def unit_hi(q, last_user=None):
                act.wait_ge(raw_loaded[q % 2], raw_loads(q, q % 2))
                if last_user is not None:
                    act.wait_ge(pe_done, last_user + 1)
                s, columns = W_SLOT[q], q < U_OUT
                for t in range(2):
                    nc.scalar.activation(half_of(w_hi[s][:, :], columns, t),
                                         half_of(raw[:, q % 2, :], columns, t), ACT.Copy).then_inc(hi_done, 1)

            act.wait_ge(small_ready, 1)
            for m in range(TT):
                act.wait_ge(x_loaded[m], 16)
                if m >= 2:
                    act.wait_ge(pe_done, J_T1[m - 2] + 1)
                norm_std(IN, m)
                if m == 0:
                    act.wait_ge(pe_done, J_CONST + 1)
                    consts = slot_of(J_CONST)
                    nc.scalar.activation(chan[:, :, :], consts[:, 0:CT * ROWS]
                                         .rearrange("p (c r) -> p c r", c=CT), ACT.Copy).then_inc(chan_ready, 1)
                    nc.scalar.activation(fchan[:, :, :], consts[:, BANK:BANK + FT * (FTAPS + 1)]
                                         .rearrange("p (c r) -> p c r", c=FT), ACT.Copy).then_inc(chan_ready, 1)
                if m >= 1:
                    transposed_hi(J_T1[m - 1], m - 1)
                if m in (2, 3):
                    unit_hi(m - 2)
            transposed_hi(J_T1[TT - 1], TT - 1)
            act.wait_ge(pool_w_loaded, 16)
            act.wait_ge(normed, TT)
            nc.scalar.activation(pw_hi[:, :, :], pw_raw, ACT.Copy).then_inc(pw_done, 1)

            def gate_sigmoid(j):
                n = J_IN[2 * j + 1]
                act.wait_ge(pe_done, n + 1)
                if j >= 2:
                    act.wait_ge(u_done, j - 1)
                nc.scalar.activation(tmp[:, j % 2, :], slot_of(n)[:, :], ACT.Sigmoid).then_inc(sig_done, 1)

            def pool_tokens(g):
                n = J_IN[2 * CT + GROUPS - 1 - g]
                act.wait_ge(pe_done, n + 1)
                nc.scalar.activation(tokens[:, g, :], slot_of(n)[:, :], ACT.Copy).then_inc(tokens_ready, 1)

            unit_hi(2)
            gate_sigmoid(0)
            unit_hi(3, J_IN[2])
            unit_hi(4, J_IN[3])
            gate_sigmoid(1)
            gate_sigmoid(2)
            unit_hi(5, J_IN[6])
            gate_sigmoid(3)
            unit_hi(6, J_IN[7])
            pool_tokens(3)
            pool_tokens(2)
            unit_hi(7, J_IN[9])
            pool_tokens(1)
            pool_tokens(0)

            def ln_z(h):
                a = h * HT
                act.wait_ge(ln_step, LN_STEPS * h + 2 * HT)
                nc.scalar.activation(std[:, LN, a:a + HT], mean_var[:, a:a + HT, 1], ACT.Sqrt,
                                     bias=eps[:, 0:1]).then_inc(ln_std_done, 1)
                act.wait_ge(ln_step, LN_STEPS * (h + 1))
                for i in range(HT):
                    bank = slice((i % 2) * BANK, (i % 2 + 1) * BANK)
                    nc.scalar.activation(tmp[:, i // 2, bank], slot_of(J_LN[h][i // 2])[:, bank], ACT.Identity,
                                         bias=shift[:, a + i:a + i + 1],
                                         scale=rstd[:, LN, a + i:a + i + 1]).then_inc(z_done, 1)

            def ln_silu(h):
                for j in range(CT):
                    n = J_BACK[h][j // 2]
                    y = slot_of(n)[:, (j % 2) * BANK:(j % 2 + 1) * BANK]
                    act.wait_ge(pe_done, n + 1)
                    nc.scalar.activation(y, y, ACT.Silu, scale=chan[:, j, LN_G:LN_G + 1],
                                         bias=chan[:, j, LN_B:LN_B + 1]).then_inc(silu_done, 1)
                    act.wait_ge(silu_done, h * CT + j + 1)
                    nc.scalar.activation(act_hi[:, j, h * HALF:(h + 1) * HALF], y,
                                         ACT.Copy).then_inc(act_hi_done, 1)

            act.wait_ge(pe_done, J_IN[-1] + 1)
            for n in range(GROUPS):
                g = GROUPS - 1 - n
                act.wait_ge(d_step, 3 * (n + 1))
                nc.scalar.activation(act_hi[:, CT + g, :], tokens[:, g, :], ACT.Copy).then_inc(act_hi_done, 1)
            ln_z(0)
            for n in range(GROUPS):
                g = GROUPS - 1 - n
                act.wait_ge(pe_done, J_POOL[n] + 1)
                nc.scalar.activation(act_hi[:, CT + g, :], slot_of(J_POOL[n])[:, :], ACT.Copy,
                                     scale=chan[:, g, SCALE:SCALE + 1]).then_inc(act_hi_done, 1)
            unit_hi(8, J_IN[2 * CT + 3])
            act.wait_ge(act_lo_done, DIFF_DONE + GROUPS)
            unit_hi(9)
            ln_silu(0)

            def ffn_hi(kind, i, t, q, par, last_user):
                act.wait_ge(raw_loaded[par], raw_loads(q, par))
                act.wait_ge(pe_done, last_user + 1)
                nc.scalar.activation(half_of(w_hi[FFN_SLOT[kind]][:, :], kind != "d", t),
                                     half_of(raw[:, par, :], kind != "d", t), ACT.Copy).then_inc(hi_done, 1)

            for m in range(TT):
                if m == HT:
                    transposed_hi(J_T2[m - 1], m - 1)
                    ln_z(1)
                    ln_silu(1)
                if m == TT - 1:
                    ffn_hi("g", 0, 0, U_FFN, 0, J_OUT[-1])
                act.wait_ge(x1_done, m + 1)
                if m >= 2:
                    act.wait_ge(pe_done, J_T2[m - 2] + 1)
                norm_std(FFN, m)
                if m % HT:
                    transposed_hi(J_T2[m - 1], m - 1)
            ffn_hi("v", 0, 0, U_FFN + 1, 1, J_OUT[-1])
            transposed_hi(J_T2[TT - 1], TT - 1)
            ffn_hi("g", 0, 1, U_FFN, 0, J_OUT[-1])
            ffn_hi("v", 0, 1, U_FFN + 1, 1, J_OUT[-1])

            def body(i, par, first=False, last=False):
                q = i * 3 + (U_FFN + 1)
                gq, vq, gpar, vpar = (q + 1, q + 2, par, 1 - par) if not first else (U_FFN + 2, U_FFN + 3, 0, 1)
                if not first:
                    before = i * BODY + (J_BODY - BODY - 1)
                    for t in range(2):
                        ffn_hi("d", i - 1, t, q, 1 - par, before)
                for t in range(2):
                    f = i * 2 + t
                    gate, value = up_job(i, 2 * t), up_job(i, 2 * t + 1)
                    c = fchan[:, f, :] if isinstance(i, int) else fchan[:, bass.ds(f, 1), :].squeeze(1)
                    act.wait_ge(pe_done, gate + 1)
                    if not first:
                        act.wait_ge(gv_lo_done, i * 2 + (t - 1))
                    nc.scalar.activation(tmp[:, t, :], slot[(J_BODY + 2 * t) % 4][:, :], ACT.Identity,
                                         scale=c[:, FTAPS - 1:FTAPS], bias=c[:, FTAPS:FTAPS + 1])\
                      .then_inc(last_tap_done, 1)
                    if not last:
                        ffn_hi("g", i + 1, t, gq, gpar, gate)
                    act.wait_ge(gate_taps, i * 2 + (t + 1))
                    nc.scalar.activation(tmp[:, t, :], tmp[:, t, :], ACT.Silu).then_inc(gate_silu, 1)
                    if not last:
                        ffn_hi("v", i + 1, t, vq, vpar, value)
                    act.wait_ge(gated, i * 2 + (t + 1))
                    nc.scalar.activation(gv_hi[:, par, t, :], tmp[:, t, :], ACT.Copy).then_inc(gv_hi_done, 1)

            body(0, 0, first=True)
            with act.Fori(1, CHUNKS - 2, 2) as i:
                body(i, 1)
                body(i + 1, 0)
            body(CHUNKS - 2, 1)
            body(CHUNKS - 1, 0, last=True)
            for t in range(2):
                ffn_hi("d", CHUNKS - 1, t, U_FFN + 3 * CHUNKS - 1, 0, down_job(CHUNKS - 2, TT - 1))
            act.wait_ge(gv_lo_done, FT)
            for m in range(TT):
                act.wait_ge(x2_done, m + 1)
                norm_std(FINAL, m)

        @block.vector
        def _(dve):
            def norm_apply(row, m, gains):
                n = row * TT + m + 1
                dve.wait_ge(std_done, n)
                nc.vector.reciprocal(rstd[:, row, m:m + 1], std[:, row, m:m + 1]).then_inc(rstd_done, 1)
                dve.wait_ge(rstd_done, n)
                dve.wait_ge(gain_loaded, 16 * gains)
                if row == FINAL:
                    if m >= 4:
                        dve.wait_ge(stored[m % 4], 16)
                    dst, done = raw[:, m % 4 // 2, (m % 2) * D:(m % 2 + 1) * D], out_ready
                else:
                    dst, done = tmp[:, m % 2, :], normed
                nc.vector.scalar_tensor_tensor(dst, x_sb[:, m, :], rstd[:, row, m:m + 1], gain[:, :],
                                               ALU.mult, ALU.mult).then_inc(done, 1)

            def transposed_lo(n, m, count):
                dve.wait_ge(act_hi_done, count)
                cols = slice(m * P, (m + 1) * P)
                nc.vector.tensor_tensor(act_lo[:, :, cols], slot_of(n)[:, :].rearrange("p (k n) -> p k n", k=KT),
                                        act_hi[:, :, cols].bitcast(F32), ALU.subtract).then_inc(act_lo_done, 1)

            def unit_lo(q):
                s, columns = W_SLOT[q], q < U_OUT
                for t in range(2):
                    dve.wait_ge(hi_done, 2 * q + t + 1)
                    nc.vector.tensor_tensor(half_of(w_lo[s][:, :], columns, t),
                                            half_of(raw[:, q % 2, :], columns, t),
                                            half_of(w_hi[s][:, :].bitcast(F32), columns, t),
                                            ALU.subtract).then_inc(lo_done, 1)

            for m in range(TT):
                norm_apply(IN, m, 1)
                if m >= 1:
                    transposed_lo(J_T1[m - 1], m - 1, T1_DONE + m)
                if m in (2, 3):
                    unit_lo(m - 2)
            transposed_lo(J_T1[TT - 1], TT - 1, T1_DONE + TT)
            dve.wait_ge(pw_done, 1)
            nc.vector.tensor_tensor(pw_lo[:, :, :], pw_raw, pw_hi[:, :, :].bitcast(F32),
                                    ALU.subtract).then_inc(pw_done, 1)

            def conv_taps(j, h, first, end):
                done = TAPS * (CT * h + j)
                for s in range(first, end):
                    tap = chan[:, j, TAPS - 1 - s:TAPS - s]
                    a, e = max(h * HALF, s), (h + 1) * HALF
                    dst = conv[:, h, j, a - h * HALF:HALF]
                    if s == 0:
                        nc.vector.tensor_scalar(dst, u[:, j, a:e], tap, chan[:, j, BIAS:BIAS + 1],
                                                ALU.mult, ALU.add).then_inc(conv_step, 1)
                    else:
                        dve.wait_ge(conv_step, done + s)
                        nc.vector.scalar_tensor_tensor(dst, u[:, j, a - s:e - s], tap, dst,
                                                       ALU.mult, ALU.add).then_inc(conv_step, 1)

            dve.wait_ge(normed, TT)
            dve.wait_ge(chan_ready, 2)
            for j in range(CT):
                dve.wait_ge(sig_done, j + 1)
                nc.vector.tensor_tensor(u[:, j, :], slot_of(J_IN[2 * j])[:, :], tmp[:, j % 2, :],
                                        ALU.mult).then_inc(u_done, 1)
                dve.wait_ge(u_done, j + 1)
                conv_taps(j, 0, 0, TAPS)

            def pool_difference(g):
                n = GROUPS - 1 - g
                w, sums = WINDOWS[g], tmp[:, g % 2, :]
                dve.wait_ge(window_step, WINDOW_STEPS[g])
                dve.wait_ge(small_ready, 1 + WINDOWS[-1])
                if n:
                    dve.wait_ge(d_step, 3 * n)
                nc.vector.tensor_tensor(edge[:, 0:w - 1], sums[:, 0:w - 1], inv_count[:, 0:w - 1],
                                        ALU.mult).then_inc(d_step, 1)
                nc.vector.scalar_tensor_tensor(tokens[:, g, w - 1:SEQ], sums[:, w - 1:SEQ], 1.0 / w,
                                               tokens[:, g, w - 1:SEQ], ALU.mult, ALU.subtract)\
                  .then_inc(d_step, 1)
                dve.wait_ge(d_step, 3 * n + 1)
                nc.vector.tensor_tensor(tokens[:, g, 0:w - 1], edge[:, 0:w - 1], tokens[:, g, 0:w - 1],
                                        ALU.subtract).then_inc(d_step, 1)

            def ln_stats(h):
                a, base = h * HT, LN_STEPS * h
                for i in range(HT):
                    n = J_LN[h][i // 2]
                    dve.wait_ge(pe_done, n + 1)
                    nc.vector.bn_stats(bn[:, a + i, :], slot_of(n)[:, (i % 2) * BANK:(i % 2 + 1) * BANK])\
                      .then_inc(ln_step, 1)
                for i in range(HT):
                    dve.wait_ge(ln_step, base + i + 1)
                    nc.vector.bn_aggr(mean_var[:, a + i, :], bn[:, a + i, :]).then_inc(ln_step, 1)
                dve.wait_ge(ln_std_done, h + 1)
                nc.vector.reciprocal(rstd[:, LN, a:a + HT], std[:, LN, a:a + HT]).then_inc(ln_step, 1)
                dve.wait_ge(ln_step, base + 2 * HT + 1)
                nc.vector.scalar_tensor_tensor(shift[:, a:a + HT], mean_var[:, a:a + HT, 0], -1.0,
                                               rstd[:, LN, a:a + HT], ALU.mult, ALU.mult).then_inc(ln_step, 1)

            def ya_lo(h):
                for j in range(CT):
                    cols = slice(h * HALF, (h + 1) * HALF)
                    dve.wait_ge(act_hi_done, YA_DONE[h] + j + 1)
                    nc.vector.tensor_tensor(act_lo[:, j, cols],
                                            slot_of(J_BACK[h][j // 2])[:, (j % 2) * BANK:(j % 2 + 1) * BANK],
                                            act_hi[:, j, cols].bitcast(F32), ALU.subtract)\
                      .then_inc(act_lo_done, 1)

            def x1(m):
                dve.wait_ge(pe_done, J_OUT[m] + 1)
                if m >= HT:
                    dve.wait_ge(x_loaded[m], 32)
                nc.vector.tensor_tensor(x_sb[:, m, :], x_sb[:, m, :], slot_of(J_OUT[m])[:, :],
                                        ALU.add).then_inc(x1_done, 1)

            def t2_lo(m):
                transposed_lo(J_T2[m], m, T2_DONE[m // HT] + m % HT + 1)

            dve.wait_ge(pw_done, 2)
            conv_taps(0, 1, 0, TAPS)
            pool_difference(3)
            pool_difference(2)
            conv_taps(1, 1, 0, 12)
            pool_difference(1)
            pool_difference(0)
            for n in range(GROUPS):
                g = GROUPS - 1 - n
                dve.wait_ge(act_hi_done, DIFF_DONE + n + 1)
                nc.vector.tensor_tensor(act_lo[:, CT + g, :], tokens[:, g, :], act_hi[:, CT + g, :].bitcast(F32),
                                        ALU.subtract).then_inc(act_lo_done, 1)
            ln_stats(0)
            conv_taps(1, 1, 12, 16)
            for n in range(GROUPS):
                g = GROUPS - 1 - n
                dve.wait_ge(act_hi_done, YB_DONE + n + 1)
                nc.vector.scalar_tensor_tensor(act_lo[:, CT + g, :], slot_of(J_POOL[n])[:, :],
                                               chan[:, g, SCALE:SCALE + 1], act_hi[:, CT + g, :].bitcast(F32),
                                               ALU.mult, ALU.subtract).then_inc(act_lo_done, 1)
            conv_taps(1, 1, 16, 20)
            ya_lo(0)
            conv_taps(1, 1, 20, TAPS)
            conv_taps(2, 1, 0, 8)
            x1(0)
            conv_taps(2, 1, 8, 11)
            norm_apply(FFN, 0, 2)
            conv_taps(2, 1, 11, 25)
            x1(1)
            t2_lo(0)
            conv_taps(2, 1, 25, 28)
            norm_apply(FFN, 1, 2)
            conv_taps(2, 1, 28, TAPS)
            conv_taps(3, 1, 0, 10)
            x1(2)
            t2_lo(1)
            conv_taps(3, 1, 10, 13)
            norm_apply(FFN, 2, 2)
            conv_taps(3, 1, 13, TAPS)
            x1(3)
            t2_lo(2)
            norm_apply(FFN, 3, 2)
            t2_lo(3)
            ln_stats(1)
            ya_lo(1)

            def ffn_lo(kind, i, t, par):
                s = FFN_SLOT[kind]
                dve.wait_ge(hi_done, ffn_half(kind, i, t) + HI0)
                nc.vector.tensor_tensor(half_of(w_lo[s][:, :], kind != "d", t),
                                        half_of(raw[:, par, :], kind != "d", t),
                                        half_of(w_hi[s][:, :].bitcast(F32), kind != "d", t),
                                        ALU.subtract).then_inc(lo_done, 1)

            for m in range(HT, TT):
                x1(m)
                if m == TT - 1:
                    ffn_lo("g", 0, 0, 0)
                norm_apply(FFN, m, 2)
                if m > HT:
                    t2_lo(m - 1)
            ffn_lo("v", 0, 0, 1)
            t2_lo(TT - 1)
            ffn_lo("g", 0, 1, 0)
            ffn_lo("v", 0, 1, 1)

            def gate(i, t):
                f = i * 2 + t
                c = fchan[:, f, :] if isinstance(i, int) else fchan[:, bass.ds(f, 1), :].squeeze(1)
                ps = slot[(J_BODY + 2 * t) % 4]
                dve.wait_ge(last_tap_done, i * 2 + (t + 1))
                for s in (1, 2):
                    if s == 2:
                        dve.wait_ge(gate_one, i * 2 + (t + 1))
                    nc.vector.scalar_tensor_tensor(tmp[:, t, s:SEQ], ps[:, 0:SEQ - s],
                                                   c[:, FTAPS - 1 - s:FTAPS - s], tmp[:, t, s:SEQ],
                                                   ALU.mult, ALU.add).then_inc(gate_one if s == 1 else gate_taps, 1)

            def gate_times_value(i, t):
                dve.wait_ge(gate_silu, i * 2 + (t + 1))
                dve.wait_ge(pe_done, up_job(i, 2 * t + 1) + 1)
                nc.vector.tensor_tensor(tmp[:, t, :], tmp[:, t, :], slot[(J_BODY + 2 * t + 1) % 4][:, :],
                                        ALU.mult).then_inc(gated, 1)

            def gv_low(i, t, par):
                dve.wait_ge(gv_hi_done, i * 2 + (t + 1))
                nc.vector.tensor_tensor(gv_lo[:, par, t, :], tmp[:, t, :], gv_hi[:, par, t, :].bitcast(F32),
                                        ALU.subtract).then_inc(gv_lo_done, 1)

            def add_down(i, m):
                dve.wait_ge(pe_done, down_job(i, m) + 1)
                if isinstance(i, int) and i == 0:
                    dve.wait_ge(normed, 2 * TT)
                else:
                    dve.wait_ge(x_added, i * TT + (m - TT + 1))
                last = isinstance(i, int) and i == CHUNKS - 1
                nc.vector.tensor_tensor(x_sb[:, m, :], x_sb[:, m, :], slot[(J_BODY + m) % 4][:, :],
                                        ALU.add).then_inc(x2_done if last else x_added, 1)

            def body(i, par, down=True, last=False):
                gpar, vpar = (par, 1 - par) if down else (0, 1)
                if down:
                    ffn_lo("d", i - 1, 0, 1 - par)
                    ffn_lo("d", i - 1, 1, 1 - par)
                gate(i, 0)
                if not last:
                    ffn_lo("g", i + 1, 0, gpar)
                gate_times_value(i, 0)
                if not last:
                    ffn_lo("v", i + 1, 0, vpar)
                gv_low(i, 0, par)
                gate(i, 1)
                if not last:
                    ffn_lo("g", i + 1, 1, gpar)
                gate_times_value(i, 1)
                if not last:
                    ffn_lo("v", i + 1, 1, vpar)
                if down:
                    add_down(i - 1, 0)
                gv_low(i, 1, par)
                if down:
                    for m in range(1, TT):
                        add_down(i - 1, m)

            body(0, 0, down=False)
            body(1, 1)
            body(2, 0)
            with dve.Fori(3, CHUNKS - 2, 2) as i:
                body(i, 1)
                body(i + 1, 0)
            body(CHUNKS - 2, 1)
            body(CHUNKS - 1, 0, last=True)
            for t in range(2):
                ffn_lo("d", CHUNKS - 1, t, 0)
            dve.wait_ge(lo_done, LO0 + ffn_half("d", CHUNKS - 1, 1))
            for m in range(TT):
                add_down(CHUNKS - 1, m)
                if m >= 1:
                    norm_apply(FINAL, m - 1, 3)
            norm_apply(FINAL, TT - 1, 3)

        @block.tensor
        def _(pe):
            def slot_read(n):
                if n >= 4:
                    pe.wait_ge(*read[n - 4])

            def three_passes(out_ap, st, mv, first, last):
                for s, v in ((0, 0), (0, 1), (1, 0)):
                    mm = nc.tensor.matmul(out_ap, st[s], mv[v], start=first and s == v == 0,
                                          stop=last and s == 1)
                return mm

            act = (act_hi, act_lo)
            bank = [slice(0, BANK), slice(BANK, 2 * BANK)]

            pe.wait_ge(ident_ready, 2)
            pe.wait_ge(consts_loaded, 16 * 7)
            ps = slot_of(J_CONST)
            for c in range(CT):
                nc.tensor.transpose(ps[:, c * ROWS:(c + 1) * ROWS], raw_rows[0:ROWS, c * P:(c + 1) * P],
                                    ident[0:ROWS, 0:ROWS])
            R = FTAPS + 1
            for c in range(FT):
                mm = nc.tensor.transpose(ps[:, BANK + c * R:BANK + (c + 1) * R],
                                         raw_frows[0:R, c * P:(c + 1) * P], ident[0:R, 0:R])
            mm.then_inc(pe_done, 1)

            def transpose_tile(n, m, count):
                slot_read(n)
                pe.wait_ge(normed, count)
                for k in range(KT):
                    mm = nc.tensor.transpose(slot_of(n)[:, k * P:(k + 1) * P], tmp[:, m % 2, k * P:(k + 1) * P],
                                             ident[:, :])
                mm.then_inc(pe_done, 1)

            for m in range(TT):
                transpose_tile(J_T1[m], m, m + 1)

            def column_tile(ps, s, t, waits):
                w = [whole(b[s][:, :], True)[:, :, t * P:(t + 1) * P] for b in (w_hi, w_lo)]
                for h in range(2):
                    if waits is not None:
                        pe.wait_ge(act_lo_done, waits[h])
                    for k in range(KT):
                        mm = three_passes(ps[:, bank[h]], [b[:, k, :] for b in w],
                                          [a[:, k, bank[h]] for a in act], k == 0, k == KT - 1)
                mm.then_inc(pe_done, 1)

            order = [(2 * (j // 2) + b, j % 2) for j in range(CT) for b in range(2)] + [(4, 1), (4, 0), (5, 1), (5, 0)]
            for n, (q, t) in enumerate(order):
                slot_read(J_IN[n])
                if q < DVE_UNITS:
                    pe.wait_ge(lo_done, 2 * q + t + 1)
                else:
                    pe.wait_ge(lo_pool_done, 2 * (q - DVE_UNITS) + t + 1)
                column_tile(slot_of(J_IN[n]), W_SLOT[q], t,
                            (T1_DONE + HT, T1_DONE + TT) if n == 0 else None)

            def ln_to_tokens(h):
                pe.wait_ge(conv_step, TAPS * CT * (h + 1))
                for b in range(2):
                    n = J_LN[h][b]
                    slot_read(n)
                    for i in range(2):
                        for j in range(CT):
                            cols = slice((2 * b + i) * P, (2 * b + i + 1) * P)
                            mm = nc.tensor.transpose(slot_of(n)[:, i * BANK + j * P:i * BANK + (j + 1) * P],
                                                     conv[:, h, j, cols], ident[:, :])
                    mm.then_inc(pe_done, 1)

            def ln_back(h):
                pe.wait_ge(z_done, HT * (h + 1))
                for b in range(2):
                    n = J_BACK[h][b]
                    slot_read(n)
                    for jj in range(2):
                        for i in range(HT):
                            at = (i % 2) * BANK + (2 * b + jj) * P
                            mm = nc.tensor.transpose(slot_of(n)[:, jj * BANK + i * P:jj * BANK + (i + 1) * P],
                                                     tmp[:, i // 2, at:at + P], ident[:, :])
                    mm.then_inc(pe_done, 1)

            ln_to_tokens(0)
            pe.wait_ge(pw_done, 2)
            for n in range(GROUPS):
                g = GROUPS - 1 - n
                slot_read(J_POOL[n])
                pe.wait_ge(act_lo_done, DIFF_DONE + n + 1)
                for h in range(2):
                    mm = three_passes(slot_of(J_POOL[n])[:, bank[h]], (pw_hi[:, g, :], pw_lo[:, g, :]),
                                      [a[:, CT + g, bank[h]] for a in act], True, True)
                mm.then_inc(pe_done, 1)
            ln_back(0)

            def out_projection(m):
                n = J_OUT[m]
                slot_read(n)
                pe.wait_ge(act_lo_done, YA_DONE[m // HT] + CT)
                cols = slice(m * P, (m + 1) * P)
                for r, k0 in enumerate(OUT_ROWS):
                    q = U_OUT + r
                    pe.wait_ge(lo_pool_done, 2 * (q - DVE_UNITS) + 2)
                    for kk in range(2):
                        for h in range(2):
                            mm = three_passes(slot_of(n)[:, bank[h]], [a[:, k0 + kk, cols] for a in act],
                                              [whole(b[W_SLOT[q]][:, :], False)[:, kk, bank[h]] for b in (w_hi, w_lo)],
                                              r == kk == 0, r == len(OUT_ROWS) - 1 and kk == 1)
                mm.then_inc(pe_done, 1)

            for m in range(TT):
                if m == HT:
                    ln_to_tokens(1)
                    ln_back(1)
                out_projection(m)
                if m % HT:
                    transpose_tile(J_T2[m - 1], m - 1, TT + m)
                if m % HT == HT - 1:
                    transpose_tile(J_T2[m], m, TT + m + 1)

            def up(i, t, kind, first=False):
                r = 2 * t + (kind == "v")
                if first:
                    slot_read(J_FFN + r)
                elif isinstance(i, int) and i == 1:
                    pe.wait_ge(gate_taps if kind == "g" else gated, t + 1)
                else:
                    pe.wait_ge(x_added, i * TT + (r + UPS - 2 * TT + 1))
                pe.wait_ge(lo_done, ffn_half(kind, i, t) + LO0)
                column_tile(slot[(J_BODY + r) % 4], FFN_SLOT[kind], t,
                            (T2_DONE[0] + HT, T2_DONE[1] + HT) if first and r == 0 else None)

            def down(i, par):
                last = isinstance(i, int) and i == CHUNKS - 1
                for m in range(TT):
                    if m < UPS:
                        if last:
                            pe.wait_ge(x_added, i * TT + (m - UPS + 1))
                        else:
                            pe.wait_ge(gated if m % 2 else gate_taps, i * 2 + (2 + m // 2 + 1))
                    else:
                        pe.wait_ge(x2_done if last else x_added, (0 if last else i * TT) + (m - UPS + 1))
                    if m == 0:
                        pe.wait_ge(lo_done, ffn_half("d", i, 1) + LO0)
                        pe.wait_ge(gv_lo_done, i * 2 + 2)
                    cols = slice(m * P, (m + 1) * P)
                    for kk in range(2):
                        for h in range(2):
                            mm = three_passes(slot[(J_BODY + m) % 4][:, bank[h]],
                                              [b[:, par, kk, cols] for b in (gv_hi, gv_lo)],
                                              [whole(b[FFN_SLOT["d"]][:, :], False)[:, kk, bank[h]]
                                               for b in (w_hi, w_lo)], kk == 0, kk == 1)
                    mm.then_inc(pe_done, 1)

            def body(i, par, first=False):
                for t in range(2):
                    up(i, t, "g", first)
                    up(i, t, "v", first)
                if not first:
                    down(i - 1, 1 - par)

            body(0, 0, first=True)
            body(1, 1)
            body(2, 0)
            with pe.Fori(3, CHUNKS - 2, 2) as i:
                body(i, 1)
                body(i + 1, 0)
            body(CHUNKS - 2, 1)
            body(CHUNKS - 1, 0)
            down(CHUNKS - 1, 0)


_INS = ["x", "norm_mix_g", "w_in", "conv_a_w", "conv_a_b", "ln_a_g", "ln_a_b", "pool_w", "pool_scale",
        "w_out", "norm_ffn_g", "w_up", "conv_f_w", "conv_f_b", "w_down", "norm_final_g"]


def kernel(**inputs):
    import numpy as np
    import concourse.bacc as bacc
    from concourse.bass_utils import run_bass_kernel_spmd

    nc = bacc.Bacc("TRN2", target_bir_lowering=False, num_devices=1)
    arrays, args = {}, []
    for name in _INS:
        a = np.ascontiguousarray(inputs[name])
        arrays[f"in_{name}"] = a
        args.append(nc.dram_tensor(f"in_{name}", a.shape, mybir.dt.from_np(a.dtype), kind="ExternalInput").ap())
    out = nc.dram_tensor("out_0", inputs["x"].shape, F32, kind="ExternalOutput").ap()
    hybrid_block(nc, *args, out)
    result = run_bass_kernel_spmd(nc, [arrays], core_ids=[0])
    return result.results[0]["out_0"]
```

```python
from contextlib import ExitStack

import concourse.bass as bass
from concourse import mybir

P = 128
BANK = 512
F32 = mybir.dt.float32
F32R = mybir.dt.float32r
ALU = mybir.AluOpType
ACT = mybir.ActivationFunctionType


def hybrid_block(nc, x, norm_mix_g, w_in, conv_a_w, conv_a_b, ln_a_g, ln_a_b, pool_w, pool_scale,
                 w_out, norm_ffn_g, w_up, conv_f_w, conv_f_b, w_down, norm_final_g, out):
    _, SEQ, D = x.shape
    DEPTH, TAPS, D_CONV = conv_a_w.shape
    GROUPS, GDIM = pool_w.shape[1:3]
    D_FF = w_down.shape[1]
    FTAPS = conv_f_w.shape[1]
    WINDOWS = (2, 4, 8, 16)
    EPS = 1e-6
    KT = D // P
    TT = SEQ // P
    HALF = SEQ // 2
    HT = TT // 2
    CT = D_CONV // P
    FT = D_FF // P
    CHUNKS = FT // 2
    W2 = 2 * P
    assert DEPTH == 1 and SEQ == D == 2 * BANK and GDIM == P and GROUPS == CT == 4
    assert FT == 2 * CHUNKS and CHUNKS % 2 == 1 and FTAPS == 3 and KT == TT == 8

    x_rows = x.rearrange("b (m p) d -> p (b m) d", p=P)
    out_rows = out.rearrange("b (m p) d -> p (b m) d", p=P)
    w_in_v = w_in[0].rearrange("(k p) n -> p k n", p=P)
    w_out_v = w_out[0].rearrange("(k p) n -> p k n", p=P)
    w_up_v = w_up[0].rearrange("(k p) n -> p k n", p=P)
    w_down_v = w_down[0].rearrange("(k p) n -> p k n", p=P)
    pool_w_v = pool_w[0].rearrange("g c d -> c g d")

    counter = [0]

    def jobs(n):
        counter[0] += n
        return list(range(counter[0] - n, counter[0]))

    SLOT, J = {}, {}
    for key, s in (
            [(("t1", 0), 3), (("t1", 1), 2), (("t1", 2), 1), (("const",), 0), (("t1", 3), 3), (("t1", 4), 2),
             (("t1", 5), 0), (("t1", 6), 3), (("t1", 7), 0)] +
            [(("in", n), (n + 1) % 4) for n in range(2 * CT + 3)] +
            [(("ln", 0, 0), 0), (("ln", 0, 1), 1), (("back", 0, 0), 3), (("back", 0, 1), 0), (("in", 2 * CT + 3), 2)] +
            [(("pool", 0), 3), (("pool", 1), 0), (("pool", 2), 3), (("pool", 3), 0)] +
            [(("out", 0), 1), (("out", 1), 2), (("t2", 0), 3), (("out", 2), 0), (("t2", 1), 1),
             (("ln", 1, 0), 2), (("ln", 1, 1), 3), (("back", 1, 0), 2), (("back", 1, 1), 3), (("out", 3), 0),
             (("t2", 2), 1), (("out", 4), 2), (("t2", 3), 3), (("out", 5), 0), (("t2", 4), 1),
             (("out", 6), 2), (("t2", 5), 3), (("out", 7), 0), (("t2", 6), 1), (("t2", 7), 0)]):
        J[key] = jobs(1)[0]
        SLOT[J[key]] = s
    J_CONST = J["const",]
    J_T1, J_OUT, J_T2 = ([J[kind, m] for m in range(TT)] for kind in ("t1", "out", "t2"))
    J_IN = [J["in", n] for n in range(2 * CT + GROUPS)]
    J_POOL = [J["pool", n] for n in range(GROUPS)]
    J_LN, J_BACK = ([[J[kind, h, b] for b in range(2)] for h in range(2)] for kind in ("ln", "back"))
    F_SLOT = 2
    UPS = 4
    J_FFN = jobs(UPS)[0]
    J_BODY = counter[0]
    BODY = UPS + TT
    SLOT |= {J_FFN + n: (F_SLOT + n) % 4 for n in range(UPS)}

    def up_job(i, r):
        return J_FFN + r if isinstance(i, int) and i == 0 else i * BODY + (J_BODY - BODY + r)

    def down_job(i, m):
        if isinstance(i, int) and i == CHUNKS - 1:
            return J_BODY + i * BODY + m
        return i * BODY + (J_BODY + UPS + m)

    IN_COLS = (0, D_CONV, W2, D_CONV + W2, 2 * D_CONV + W2, 2 * D_CONV)
    OUT_ROWS = (0, 2, 4, 6)
    U_OUT = len(IN_COLS)
    U_FFN = U_OUT + len(OUT_ROWS)
    W_SLOT = (0, 1, 2, 0, 1, 2, 0, 1, 2, 3)
    FFN_SLOT = {"g": 0, "v": 1, "d": 2}
    POOL_UNITS = 2
    HI0, LO0 = 2 * U_FFN, 2 * (U_FFN - POOL_UNITS)

    def ffn_half(kind, i, t):
        if kind == "d":
            return 6 * (CHUNKS - 1) + 5 + t if isinstance(i, int) and i == CHUNKS - 1 else i * 6 + (9 + t)
        o = 2 * t + (kind == "v")
        return 1 + o if isinstance(i, int) and i == 0 else i * 6 + (o - 1)

    def raw_loads(q, par):
        return q * 8 + (16 - 8 * par)

    with ExitStack() as ctx:
        def sb(name, shape, dt=F32):
            return ctx.enter_context(nc.sbuf_tensor(name, shape, dt))

        def sem(name):
            return ctx.enter_context(nc.semaphore(name))

        ROWS = TAPS + 4
        BIAS, LN_G, LN_B, SCALE = range(TAPS, ROWS)
        x_sb = sb("x_sb", [P, TT, D])
        act_hi = sb("act_hi", [P, KT, SEQ], F32R)
        act_lo = sb("act_lo", [P, KT, SEQ], F32R)
        raw = sb("raw", [P, 2, 2 * D])
        w_hi = [sb(f"w_hi{s}", [P, 2 * D], F32R) for s in range(3)]
        w_lo = [sb(f"w_lo{s}", [P, 2 * D], F32R) for s in range(3)]
        tmp = sb("tmp", [P, 2, SEQ])
        z_sb = sb("z_sb", [P, 2, SEQ])
        RING = 4
        prod = sb("prod", [P, RING, HALF])
        ident = sb("ident", [P, P])
        chan = sb("chan", [P, CT, ROWS])
        fchan = sb("fchan", [P, FT, FTAPS + 1])
        inv_count = sb("inv_count", [P, WINDOWS[-1]])
        edge = sb("edge", [P, WINDOWS[-1]])
        eps = sb("eps", [P, 1])
        IN, FFN, FINAL, LN = range(4)
        sumsq = sb("sumsq", [P, 3, TT])
        std = sb("std", [P, 4, TT])
        rstd = sb("rstd", [P, 4, TT])
        bn = sb("bn", [P, TT, 6])
        mean_var = sb("mean_var", [P, TT, 2])
        shift = sb("shift", [P, TT])
        with nc.sbuf_tensor("pw_hi", [P, GROUPS, P], F32R) as pw_hi:
            with nc.sbuf_tensor("pw_lo", [P, GROUPS, P], F32R) as pw_lo:
                pass
        gain = sb("gain", [P, D])
        with nc.sbuf_tensor("conv", [P, 2, CT, HALF], F32) as conv:
            with nc.sbuf_tensor("tokens", [P, GROUPS, SEQ], F32) as tokens:
                pass
            with nc.sbuf_tensor("w_hi3", [P, 2 * D], F32R) as w_hi3:
                with nc.sbuf_tensor("w_lo3", [P, 2 * D], F32R) as w_lo3:
                    pass
        gv_hi = sb("gv_hi", [P, 2, 2, SEQ], F32R)
        gv_lo = sb("gv_lo", [P, 2, 2, SEQ], F32R)
        w_hi.append(w_hi3)
        w_lo.append(w_lo3)
        raw_rows = conv[:, 0, 0, :]
        raw_frows = tokens[:, :, :].rearrange("p a b -> p (a b)")[:, 0:D_FF]
        pw_raw = conv[:, 1, 0, :].rearrange("p (g d) -> p g d", g=GROUPS)
        u = x_sb[:, HT:TT, :]

        slot = [ctx.enter_context(nc.psum_tensor(f"slot{s}", [P, 2 * BANK], F32)) for s in range(4)]

        def slot_of(n):
            return slot[SLOT[n]]

        consts_loaded = sem("consts_loaded")
        pool_w_loaded = sem("pool_w_loaded")
        gain_loaded = sem("gain_loaded")
        x_loaded = [sem(f"x_loaded{m}") for m in range(TT)]
        raw_loaded = [sem(f"raw_loaded{b}") for b in range(2)]
        stored = [sem(f"stored{b}") for b in range(4)]
        ident_ready = sem("ident_ready")
        small_ready = sem("small_ready")
        pe_done = sem("pe_done")
        chan_ready = sem("chan_ready")
        hi_done = sem("hi_done")
        lo_done = sem("lo_done")
        lo_pool_done = sem("lo_pool_done")
        pw_done = sem("pw_done")
        squares_done = sem("squares_done")
        std_done = sem("std_done")
        rstd_done = sem("rstd_done")
        normed = sem("normed")
        act_hi_done = sem("act_hi_done")
        act_lo_done = sem("act_lo_done")
        sig_done = sem("sig_done")
        u_done = sem("u_done")
        first_tap_done = sem("first_tap_done")
        product_done = sem("product_done")
        light_step = sem("light_step")
        conv_step = sem("conv_step")
        conv_done = [sem(f"conv_done{h}") for h in range(2)]
        out_used = sem("out_used")
        tokens_ready = sem("tokens_ready")
        window_step = sem("window_step")
        d_step = sem("d_step")
        ln_step = sem("ln_step")
        ln_std_done = sem("ln_std_done")
        z_done = sem("z_done")
        silu_done = sem("silu_done")
        x1_done = sem("x1_done")
        last_tap_done = sem("last_tap_done")
        gate_one = sem("gate_one")
        gate_taps = sem("gate_taps")
        gate_silu = sem("gate_silu")
        gated = sem("gated")
        gv_hi_done = sem("gv_hi_done")
        gv_lo_done = sem("gv_lo_done")
        x_added = sem("x_added")
        x2_done = sem("x2_done")
        out_ready = sem("out_ready")

        PIECES = ([("t1", m) for m in range(TT)] + [("ya", 0, j) for j in range(CT)] +
                  [("diff", n) for n in range(GROUPS)] + [("yb", n) for n in range(GROUPS)] +
                  [("t2", m) for m in range(HT - 2)] + [("ya", 1, j) for j in range(CT)] +
                  [("t2", m) for m in range(HT - 2, TT)])
        DONE = {piece: n + 1 for n, piece in enumerate(PIECES)}

        LIGHT = {(0, 1): 15, (1, 0): 14, (2, 0): 14, (3, 0): 6, (1, 1): 12, (2, 1): 12, (3, 1): 13}
        light_before, light_first = {}, {}
        for jh in LIGHT:
            light_first[jh] = len(light_first)
            light_before[jh] = sum(LIGHT[b] - 1 for b in light_before)

        WINDOW_STEPS = [sum(2 * (k + 1) for k in range(g, GROUPS)) for g in range(GROUPS)]
        LN_STEPS = 2 * HT + 2

        read = {J_CONST: (chan_ready, 2)}
        read |= {J_T1[m]: (act_lo_done, DONE["t1", m]) for m in range(TT)}
        for j in range(CT):
            read[J_IN[2 * j]] = (u_done, j + 1)
            read[J_IN[2 * j + 1]] = (sig_done, j + 1)
            read[J_IN[2 * CT + j]] = (tokens_ready, j + 1)
            read[J_POOL[j]] = (act_lo_done, DONE["yb", j])
        for h in range(2):
            for b in range(2):
                read[J_LN[h][b]] = (z_done, HT * h + 2 * b + 2)
                read[J_BACK[h][b]] = (act_lo_done, DONE["ya", h, 2 * b + 1])
        for m in range(TT):
            read[J_OUT[m]] = (x1_done, m + 1)
            read[J_T2[m]] = (act_lo_done, DONE["t2", m])

        def half_of(buf, columns, t):
            if columns:
                return buf.rearrange("p (k n) -> p k n", k=KT)[:, :, t * P:(t + 1) * P]
            return buf[:, t * D:(t + 1) * D]

        def whole(buf, columns):
            return buf.rearrange("p (k n) -> p k n", k=KT if columns else 2)

        block = ctx.enter_context(nc.Block())

        @block.sync
        def _(sp):
            def load_x(m):
                sp.dma_start(x_sb[:, m, :], x_rows[:, m, :]).then_inc(x_loaded[m], 16)

            def load_gain(src):
                sp.dma_start(gain[:, :], src.broadcast_to([P, D])).then_inc(gain_loaded, 16)

            def load_unit(q):
                if q >= 2 + POOL_UNITS:
                    sp.wait_ge(lo_done, 2 * (q - 2 - POOL_UNITS) + 2)
                elif q >= 2:
                    sp.wait_ge(lo_pool_done, 2 * (q - 2) + 2)
                if q < U_OUT:
                    src = w_in_v[:, :, IN_COLS[q]:IN_COLS[q] + W2]
                else:
                    src = w_out_v[:, OUT_ROWS[q - U_OUT]:OUT_ROWS[q - U_OUT] + 2, :]
                sp.dma_start(whole(raw[:, q % 2, :], q < U_OUT), src).then_inc(raw_loaded[q % 2], 16)

            def load_ffn(kind, i, par):
                if kind == "d":
                    src = w_down_v[:, bass.ds(i * 2, 2), :]
                else:
                    src = w_up_v[:, :, bass.ds(i * W2 + (D_FF if kind == "v" else 0), W2)]
                sp.dma_start(whole(raw[:, par, :], kind != "d"), src).then_inc(raw_loaded[par], 16)

            load_x(0)
            load_gain(norm_mix_g)
            for m in range(1, HT):
                load_x(m)
            load_unit(0)
            load_x(HT)
            load_unit(1)
            for m in range(HT + 1, TT):
                load_x(m)
            for q in range(2, U_FFN):
                load_unit(q)
            sp.wait_ge(pe_done, J_POOL[-1] + 1)
            load_gain(norm_ffn_g)
            sp.wait_ge(lo_done, LO0 - 2)
            load_ffn("g", 0, 0)
            sp.wait_ge(lo_done, LO0)
            load_ffn("v", 0, 1)
            for j in range(CT):
                for h in range(2):
                    sp.wait_ge(conv_done[h], j + 1)
                load_x(HT + j)
            sp.wait_ge(lo_done, LO0 + ffn_half("g", 0, 1))
            load_ffn("g", 1, 0)
            sp.wait_ge(lo_done, LO0 + ffn_half("v", 0, 1))
            load_ffn("v", 1, 1)

            def body(i, par, last=False):
                sp.wait_ge(lo_done, ffn_half("g", i, 1) + LO0)
                load_ffn("d", i - 1, par)
                if not last:
                    sp.wait_ge(lo_done, ffn_half("v", i, 1) + LO0)
                    load_ffn("g", i + 1, 1 - par)
                    sp.wait_ge(lo_done, ffn_half("d", i - 1, 1) + LO0)
                    load_ffn("v", i + 1, par)

            with sp.Fori(1, CHUNKS - 2, 2) as i:
                body(i, 0)
                body(i + 1, 1)
            body(CHUNKS - 2, 0)
            body(CHUNKS - 1, 1, last=True)
            sp.wait_ge(lo_done, LO0 + ffn_half("v", CHUNKS - 1, 1))
            load_ffn("d", CHUNKS - 1, 0)
            sp.wait_ge(normed, 2 * TT)
            load_gain(norm_final_g.rearrange("(a d) -> a d", a=1))
            for m in range(TT):
                sp.wait_ge(out_ready, m + 1)
                sp.dma_start(out_rows[:, m, :], raw[:, m % 4 // 2, (m % 2) * D:(m % 2 + 1) * D])\
                  .then_inc(stored[m % 4], 16)
            for b in range(4):
                sp.wait_ge(stored[b], 16 * TT // 4)

        @block.gpsimd
        def _(pool):
            nc.gpsimd.memset(ident[:, :], 0.0).then_inc(ident_ready, 1)
            pool.wait_ge(ident_ready, 1)
            nc.gpsimd.affine_select(out=ident[:, :], in_=ident[:, :], compare_op=ALU.not_equal, fill=1.0,
                                    base=0, pattern=[[-1, P]], channel_multiplier=1).then_inc(ident_ready, 1)
            nc.gpsimd.memset(eps[:, :], EPS).then_inc(small_ready, 1)
            for t in range(WINDOWS[-1]):
                nc.gpsimd.memset(inv_count[:, t:t + 1], 1.0 / (t + 1)).then_inc(small_ready, 1)

            def unit_lo(q):
                s, columns = W_SLOT[q], q < U_OUT
                for t in range(2):
                    pool.wait_ge(hi_done, 2 * q + t + 1)
                    nc.gpsimd.tensor_tensor(half_of(w_lo[s][:, :], columns, t),
                                            half_of(raw[:, q % 2, :], columns, t),
                                            half_of(w_hi[s][:, :].bitcast(F32), columns, t),
                                            ALU.subtract).then_inc(lo_pool_done, 1)

            def windows(g, before):
                pool.wait_ge(tokens_ready, GROUPS - g)
                if g == GROUPS - 1:
                    pool.wait_ge(u_done, CT)
                else:
                    pool.wait_ge(d_step, 3 * (GROUPS - 1 - g))
                src = tokens[:, g, :]
                for b in range(g + 1):
                    w, dst = 2 ** b, tmp[:, b % 2, :]
                    if b:
                        pool.wait_ge(window_step, before + 2 * b)
                    nc.gpsimd.tensor_tensor(dst[:, w:SEQ], src[:, w:SEQ], src[:, 0:SEQ - w],
                                            ALU.add).then_inc(window_step, 1)
                    nc.gpsimd.tensor_copy(dst[:, 0:w], src[:, 0:w]).then_inc(window_step, 1)
                    src = dst

            def light_taps(j, h, first=1, end=TAPS):
                pool.wait_ge(first_tap_done, light_first[j, h] + 1)
                for s in range(first, min(end, LIGHT[j, h])):
                    n = light_before[j, h] + s - 1
                    pool.wait_ge(product_done, n + 1)
                    if s > 1:
                        pool.wait_ge(light_step, n)
                    dst = conv[:, h, j, (s if h == 0 else 0):HALF]
                    nc.gpsimd.tensor_tensor(dst, dst, prod[:, n % RING, (s if h == 0 else 0):HALF],
                                            ALU.add).then_inc(light_step, 1)

            for q in range(POOL_UNITS):
                unit_lo(q)
            light_taps(0, 1)
            light_taps(1, 0)
            light_taps(2, 0)
            light_taps(3, 0)
            windows(3, 0)
            windows(2, WINDOW_STEPS[3])
            light_taps(1, 1, 1, 5)
            windows(1, WINDOW_STEPS[2])
            light_taps(1, 1, 5, 9)
            windows(0, WINDOW_STEPS[1])
            light_taps(1, 1, 9)
            light_taps(2, 1)
            light_taps(3, 1)

        @block.scalar
        def _(act):
            act.dma_start(raw_rows[0:TAPS, :], conv_a_w[0]).then_inc(consts_loaded, 16)
            for r, v in ((BIAS, conv_a_b), (LN_G, ln_a_g), (LN_B, ln_a_b), (SCALE, pool_scale)):
                act.dma_start(raw_rows[r:r + 1, :], v).then_inc(consts_loaded, 16)
            act.dma_start(raw_frows[0:FTAPS, :], conv_f_w[0]).then_inc(consts_loaded, 16)
            act.dma_start(raw_frows[FTAPS:FTAPS + 1, :], conv_f_b).then_inc(consts_loaded, 16)
            act.dma_start(pw_raw, pool_w_v).then_inc(pool_w_loaded, 16)

            def norm_std(row, m):
                n = row * TT + m + 1
                act.wait_ge(squares_done, n - 1)
                squares = (z_sb if row == IN else tmp)[:, m % 2, :]
                nc.scalar.activation(squares, x_sb[:, m, :], ACT.Square,
                                     accum_out=sumsq[:, row, m:m + 1]).then_inc(squares_done, 1)
                act.wait_ge(squares_done, n)
                nc.scalar.activation(std[:, row, m:m + 1], sumsq[:, row, m:m + 1], ACT.Sqrt,
                                     bias=eps[:, 0:1], scale=1.0 / D).then_inc(std_done, 1)

            def transposed_hi(n, m):
                act.wait_ge(pe_done, n + 1)
                nc.scalar.activation(act_hi[:, :, m * P:(m + 1) * P],
                                     slot_of(n)[:, :].rearrange("p (k n) -> p k n", k=KT),
                                     ACT.Copy).then_inc(act_hi_done, 1)

            def unit_hi(q, last_user=None):
                act.wait_ge(raw_loaded[q % 2], raw_loads(q, q % 2))
                if last_user is not None:
                    act.wait_ge(pe_done, last_user + 1)
                s, columns = W_SLOT[q], q < U_OUT
                for t in range(2):
                    nc.scalar.activation(half_of(w_hi[s][:, :], columns, t),
                                         half_of(raw[:, q % 2, :], columns, t), ACT.Copy).then_inc(hi_done, 1)

            act.wait_ge(small_ready, 1)
            for m in range(TT):
                act.wait_ge(x_loaded[m], 16)
                norm_std(IN, m)
                if m >= 1:
                    transposed_hi(J_T1[m - 1], m - 1)
                if m == 3:
                    act.wait_ge(pe_done, J_CONST + 1)
                    consts = slot_of(J_CONST)
                    nc.scalar.activation(chan[:, :, :], consts[:, 0:CT * ROWS]
                                         .rearrange("p (c r) -> p c r", c=CT), ACT.Copy).then_inc(chan_ready, 1)
                    nc.scalar.activation(fchan[:, :, :], consts[:, BANK:BANK + FT * (FTAPS + 1)]
                                         .rearrange("p (c r) -> p c r", c=FT), ACT.Copy).then_inc(chan_ready, 1)
                if m in (4, 5):
                    unit_hi(m - 4)
            transposed_hi(J_T1[TT - 1], TT - 1)
            act.wait_ge(pool_w_loaded, 16)
            act.wait_ge(normed, TT)
            nc.scalar.activation(pw_hi[:, :, :], pw_raw, ACT.Copy).then_inc(pw_done, 1)

            def gate_sigmoid(j):
                n = J_IN[2 * j + 1]
                act.wait_ge(pe_done, n + 1)
                if j >= 2:
                    act.wait_ge(u_done, j - 1)
                nc.scalar.activation(tmp[:, j % 2, :], slot_of(n)[:, :], ACT.Sigmoid).then_inc(sig_done, 1)

            def pool_tokens(g):
                n = J_IN[2 * CT + GROUPS - 1 - g]
                act.wait_ge(pe_done, n + 1)
                nc.scalar.activation(tokens[:, g, :], slot_of(n)[:, :], ACT.Copy).then_inc(tokens_ready, 1)

            def light_products(j, h, first=0, end=TAPS):
                if first == 0:
                    act.wait_ge(u_done, j + 1)
                    nc.scalar.activation(conv[:, h, j, :], u[:, j, h * HALF:(h + 1) * HALF], ACT.Identity,
                                         scale=chan[:, j, TAPS - 1:TAPS], bias=chan[:, j, BIAS:BIAS + 1])\
                      .then_inc(first_tap_done, 1)
                for s in range(max(first, 1), min(end, LIGHT[j, h])):
                    n = light_before[j, h] + s - 1
                    if n >= RING:
                        act.wait_ge(light_step, n - RING + 1)
                    a = max(h * HALF, s)
                    nc.scalar.activation(prod[:, n % RING, a - h * HALF:HALF], u[:, j, a - s:(h + 1) * HALF - s],
                                         ACT.Copy, scale=chan[:, j, TAPS - 1 - s:TAPS - s]).then_inc(product_done, 1)

            def ln_z(h):
                a = h * HT
                act.wait_ge(ln_step, LN_STEPS * h + 2 * HT)
                nc.scalar.activation(std[:, LN, a:a + HT], mean_var[:, a:a + HT, 1], ACT.Sqrt,
                                     bias=eps[:, 0:1]).then_inc(ln_std_done, 1)
                act.wait_ge(ln_step, LN_STEPS * (h + 1))
                for i in range(HT):
                    bank = slice((i % 2) * BANK, (i % 2 + 1) * BANK)
                    nc.scalar.activation(z_sb[:, i // 2, bank], slot_of(J_LN[h][i // 2])[:, bank], ACT.Identity,
                                         bias=shift[:, a + i:a + i + 1],
                                         scale=rstd[:, LN, a + i:a + i + 1]).then_inc(z_done, 1)

            def ln_silu(h):
                for j in range(CT):
                    n = J_BACK[h][j // 2]
                    y = slot_of(n)[:, (j % 2) * BANK:(j % 2 + 1) * BANK]
                    act.wait_ge(pe_done, n + 1)
                    nc.scalar.activation(y, y, ACT.Silu, scale=chan[:, j, LN_G:LN_G + 1],
                                         bias=chan[:, j, LN_B:LN_B + 1]).then_inc(silu_done, 1)
                    act.wait_ge(silu_done, h * CT + j + 1)
                    nc.scalar.activation(act_hi[:, j, h * HALF:(h + 1) * HALF], y,
                                         ACT.Copy).then_inc(act_hi_done, 1)

            unit_hi(2)
            gate_sigmoid(0)
            act.wait_ge(pw_done, 2)
            light_products(0, 1, 0, 9)
            unit_hi(3, J_IN[2])
            light_products(0, 1, 9)
            gate_sigmoid(1)
            unit_hi(4, J_IN[3])
            light_products(1, 0)
            gate_sigmoid(2)
            light_products(2, 0, 0, 8)
            unit_hi(5, J_IN[6])
            light_products(2, 0, 8)
            gate_sigmoid(3)
            light_products(3, 0)
            unit_hi(6, J_IN[7])
            pool_tokens(3)
            pool_tokens(2)
            unit_hi(7, J_IN[9])
            light_products(1, 1, 0, 5)
            pool_tokens(1)
            ln_z(0)
            light_products(1, 1, 5, 9)
            ln_silu(0)
            pool_tokens(0)
            light_products(1, 1, 9)
            for n in range(GROUPS):
                g = GROUPS - 1 - n
                act.wait_ge(d_step, 3 * (n + 1))
                nc.scalar.activation(act_hi[:, CT + g, :], tokens[:, g, :], ACT.Copy).then_inc(act_hi_done, 1)
            unit_hi(8, J_IN[2 * CT + 3])
            light_products(2, 1, 0, 5)
            act.wait_ge(act_lo_done, DONE["diff", GROUPS - 1])
            unit_hi(9)

            def pool_output(n):
                g = GROUPS - 1 - n
                act.wait_ge(pe_done, J_POOL[n] + 1)
                nc.scalar.activation(act_hi[:, CT + g, :], slot_of(J_POOL[n])[:, :], ACT.Copy,
                                     scale=chan[:, g, SCALE:SCALE + 1]).then_inc(act_hi_done, 1)

            pool_output(0)
            pool_output(1)
            light_products(2, 1, 5, 9)
            pool_output(2)
            pool_output(3)
            light_products(2, 1, 9)
            light_products(3, 1)

            def ffn_hi(kind, i, t, q, par, last_user=None):
                act.wait_ge(raw_loaded[par], raw_loads(q, par))
                if last_user is not None:
                    act.wait_ge(pe_done, last_user + 1)
                nc.scalar.activation(half_of(w_hi[FFN_SLOT[kind]][:, :], kind != "d", t),
                                     half_of(raw[:, par, :], kind != "d", t), ACT.Copy).then_inc(hi_done, 1)

            def t2_std(m):
                act.wait_ge(x1_done, m + 1)
                if m >= 2:
                    act.wait_ge(pe_done, J_T2[m - 2] + 1)
                norm_std(FFN, m)

            t2_std(0)
            t2_std(1)
            transposed_hi(J_T2[0], 0)
            t2_std(2)
            transposed_hi(J_T2[1], 1)
            ln_z(1)
            ln_silu(1)
            for m in range(HT - 1, TT):
                t2_std(m)
                transposed_hi(J_T2[m - 1], m - 1)
                if m == TT - 2:
                    act.wait_ge(out_used, 1)
                    ffn_hi("g", 0, 0, U_FFN, 0)
                    act.wait_ge(out_used, 2)
                    ffn_hi("v", 0, 0, U_FFN + 1, 1)
            transposed_hi(J_T2[TT - 1], TT - 1)
            ffn_hi("g", 0, 1, U_FFN, 0)
            ffn_hi("v", 0, 1, U_FFN + 1, 1)

            def body(i, par, first=False, last=False):
                q = i * 3 + (U_FFN + 1)
                gq, vq, gpar, vpar = (q + 1, q + 2, par, 1 - par) if not first else (U_FFN + 2, U_FFN + 3, 0, 1)
                if not first:
                    before = i * BODY + (J_BODY - BODY - 1)
                    for t in range(2):
                        ffn_hi("d", i - 1, t, q, 1 - par, before)
                for t in range(2):
                    f = i * 2 + t
                    gate, value = up_job(i, 2 * t), up_job(i, 2 * t + 1)
                    c = fchan[:, f, :] if isinstance(i, int) else fchan[:, bass.ds(f, 1), :].squeeze(1)
                    act.wait_ge(pe_done, gate + 1)
                    if not first:
                        act.wait_ge(gv_lo_done, i * 2 + (t - 1))
                    nc.scalar.activation(tmp[:, t, :], slot[(F_SLOT + 2 * t) % 4][:, :], ACT.Identity,
                                         scale=c[:, FTAPS - 1:FTAPS], bias=c[:, FTAPS:FTAPS + 1])\
                      .then_inc(last_tap_done, 1)
                    if not last:
                        ffn_hi("g", i + 1, t, gq, gpar, gate)
                    act.wait_ge(gate_taps, i * 2 + (t + 1))
                    nc.scalar.activation(tmp[:, t, :], tmp[:, t, :], ACT.Silu).then_inc(gate_silu, 1)
                    if not last:
                        ffn_hi("v", i + 1, t, vq, vpar, value)
                    act.wait_ge(gated, i * 2 + (t + 1))
                    nc.scalar.activation(gv_hi[:, par, t, :], tmp[:, t, :], ACT.Copy).then_inc(gv_hi_done, 1)

            body(0, 0, first=True)
            with act.Fori(1, CHUNKS - 2, 2) as i:
                body(i, 1)
                body(i + 1, 0)
            body(CHUNKS - 2, 1)
            body(CHUNKS - 1, 0, last=True)
            for t in range(2):
                ffn_hi("d", CHUNKS - 1, t, U_FFN + 3 * CHUNKS - 1, 0, down_job(CHUNKS - 2, TT - 1))
            act.wait_ge(gv_lo_done, FT)
            for m in range(TT):
                act.wait_ge(x2_done, m + 1)
                norm_std(FINAL, m)

        @block.vector
        def _(dve):
            def norm_apply(row, m, gains):
                n = row * TT + m + 1
                dve.wait_ge(std_done, n)
                nc.vector.reciprocal(rstd[:, row, m:m + 1], std[:, row, m:m + 1]).then_inc(rstd_done, 1)
                dve.wait_ge(rstd_done, n)
                dve.wait_ge(gain_loaded, 16 * gains)
                if row == FINAL:
                    if m >= 4:
                        dve.wait_ge(stored[m % 4], 16)
                    dst, done = raw[:, m % 4 // 2, (m % 2) * D:(m % 2 + 1) * D], out_ready
                else:
                    dst, done = tmp[:, m % 2, :], normed
                nc.vector.scalar_tensor_tensor(dst, x_sb[:, m, :], rstd[:, row, m:m + 1], gain[:, :],
                                               ALU.mult, ALU.mult).then_inc(done, 1)

            def transposed_lo(n, m, count):
                dve.wait_ge(act_hi_done, count)
                cols = slice(m * P, (m + 1) * P)
                nc.vector.tensor_tensor(act_lo[:, :, cols], slot_of(n)[:, :].rearrange("p (k n) -> p k n", k=KT),
                                        act_hi[:, :, cols].bitcast(F32), ALU.subtract).then_inc(act_lo_done, 1)

            def unit_lo(q):
                s, columns = W_SLOT[q], q < U_OUT
                for t in range(2):
                    dve.wait_ge(hi_done, 2 * q + t + 1)
                    nc.vector.tensor_tensor(half_of(w_lo[s][:, :], columns, t),
                                            half_of(raw[:, q % 2, :], columns, t),
                                            half_of(w_hi[s][:, :].bitcast(F32), columns, t),
                                            ALU.subtract).then_inc(lo_done, 1)

            for m in range(TT):
                norm_apply(IN, m, 1)
                if m >= 1:
                    transposed_lo(J_T1[m - 1], m - 1, DONE["t1", m - 1])
            transposed_lo(J_T1[TT - 1], TT - 1, DONE["t1", TT - 1])
            dve.wait_ge(pw_done, 1)
            nc.vector.tensor_tensor(pw_lo[:, :, :], pw_raw, pw_hi[:, :, :].bitcast(F32),
                                    ALU.subtract).then_inc(pw_done, 1)

            taps_made = {}
            conv_count = [0]
            last_step = {}

            def one_tap(j, h):
                s = taps_made.get((j, h), LIGHT.get((j, h), 0))
                taps_made[j, h] = s + 1
                tap = chan[:, j, TAPS - 1 - s:TAPS - s]
                a, e = max(h * HALF, s), (h + 1) * HALF
                dst = conv[:, h, j, a - h * HALF:HALF]
                if s == 0:
                    op = nc.vector.tensor_scalar(dst, u[:, j, a:e], tap, chan[:, j, BIAS:BIAS + 1],
                                                 ALU.mult, ALU.add)
                else:
                    if s == LIGHT.get((j, h)):
                        dve.wait_ge(light_step, light_before[j, h] + s - 1)
                    else:
                        dve.wait_ge(conv_step, last_step[j, h])
                    op = nc.vector.scalar_tensor_tensor(dst, u[:, j, a - s:e - s], tap, dst, ALU.mult, ALU.add)
                if s == TAPS - 1:
                    op.then_inc(conv_done[h], 1)
                else:
                    op.then_inc(conv_step, 1)
                    conv_count[0] += 1
                    last_step[j, h] = conv_count[0]

            def conv_taps(*runs):
                for n in range(max(r[2] for r in runs)):
                    for j, h, count in runs:
                        if n < count:
                            one_tap(j, h)

            def make_u(j):
                dve.wait_ge(sig_done, j + 1)
                nc.vector.tensor_tensor(u[:, j, :], slot_of(J_IN[2 * j])[:, :], tmp[:, j % 2, :],
                                        ALU.mult).then_inc(u_done, 1)

            def pool_difference(g):
                n = GROUPS - 1 - g
                w, sums = WINDOWS[g], tmp[:, g % 2, :]
                dve.wait_ge(window_step, WINDOW_STEPS[g])
                dve.wait_ge(small_ready, 1 + WINDOWS[-1])
                if n:
                    dve.wait_ge(d_step, 3 * n)
                nc.vector.tensor_tensor(edge[:, 0:w - 1], sums[:, 0:w - 1], inv_count[:, 0:w - 1],
                                        ALU.mult).then_inc(d_step, 1)
                nc.vector.scalar_tensor_tensor(tokens[:, g, w - 1:SEQ], sums[:, w - 1:SEQ], 1.0 / w,
                                               tokens[:, g, w - 1:SEQ], ALU.mult, ALU.subtract)\
                  .then_inc(d_step, 1)
                dve.wait_ge(d_step, 3 * n + 1)
                nc.vector.tensor_tensor(tokens[:, g, 0:w - 1], edge[:, 0:w - 1], tokens[:, g, 0:w - 1],
                                        ALU.subtract).then_inc(d_step, 1)

            def ln_stats(h):
                a, base = h * HT, LN_STEPS * h
                for i in range(HT):
                    n = J_LN[h][i // 2]
                    dve.wait_ge(pe_done, n + 1)
                    nc.vector.bn_stats(bn[:, a + i, :], slot_of(n)[:, (i % 2) * BANK:(i % 2 + 1) * BANK])\
                      .then_inc(ln_step, 1)
                for i in range(HT):
                    dve.wait_ge(ln_step, base + i + 1)
                    nc.vector.bn_aggr(mean_var[:, a + i, :], bn[:, a + i, :]).then_inc(ln_step, 1)
                dve.wait_ge(ln_std_done, h + 1)
                nc.vector.reciprocal(rstd[:, LN, a:a + HT], std[:, LN, a:a + HT]).then_inc(ln_step, 1)
                dve.wait_ge(ln_step, base + 2 * HT + 1)
                nc.vector.scalar_tensor_tensor(shift[:, a:a + HT], mean_var[:, a:a + HT, 0], -1.0,
                                               rstd[:, LN, a:a + HT], ALU.mult, ALU.mult).then_inc(ln_step, 1)

            def ya_lo(h):
                for j in range(CT):
                    cols = slice(h * HALF, (h + 1) * HALF)
                    dve.wait_ge(act_hi_done, DONE["ya", h, j])
                    nc.vector.tensor_tensor(act_lo[:, j, cols],
                                            slot_of(J_BACK[h][j // 2])[:, (j % 2) * BANK:(j % 2 + 1) * BANK],
                                            act_hi[:, j, cols].bitcast(F32), ALU.subtract)\
                      .then_inc(act_lo_done, 1)

            def x1(m):
                dve.wait_ge(pe_done, J_OUT[m] + 1)
                if m >= HT:
                    dve.wait_ge(x_loaded[m], 32)
                nc.vector.tensor_tensor(x_sb[:, m, :], x_sb[:, m, :], slot_of(J_OUT[m])[:, :],
                                        ALU.add).then_inc(x1_done, 1)

            def t2_lo(m):
                transposed_lo(J_T2[m], m, DONE["t2", m])

            def difference_lo(n):
                g = GROUPS - 1 - n
                dve.wait_ge(act_hi_done, DONE["diff", n])
                nc.vector.tensor_tensor(act_lo[:, CT + g, :], tokens[:, g, :], act_hi[:, CT + g, :].bitcast(F32),
                                        ALU.subtract).then_inc(act_lo_done, 1)

            def yb_lo(n):
                g = GROUPS - 1 - n
                dve.wait_ge(act_hi_done, DONE["yb", n])
                nc.vector.scalar_tensor_tensor(act_lo[:, CT + g, :], slot_of(J_POOL[n])[:, :],
                                               chan[:, g, SCALE:SCALE + 1], act_hi[:, CT + g, :].bitcast(F32),
                                               ALU.mult, ALU.subtract).then_inc(act_lo_done, 1)

            unit_lo(2)
            dve.wait_ge(normed, TT)
            dve.wait_ge(chan_ready, 2)
            make_u(0)
            dve.wait_ge(u_done, 1)
            conv_taps((0, 0, 20))
            unit_lo(3)
            conv_taps((0, 0, 2))
            make_u(1)
            unit_lo(4)
            dve.wait_ge(u_done, 2)
            conv_taps((0, 0, 9), (0, 1, 14))
            make_u(2)
            dve.wait_ge(u_done, 3)
            conv_taps((1, 0, 17), (0, 1, 2))
            unit_lo(5)
            make_u(3)
            dve.wait_ge(u_done, 4)
            conv_taps((2, 0, 8))
            conv_taps((2, 0, 9), (3, 0, 9))
            pool_difference(3)
            conv_taps((3, 0, 16))
            unit_lo(6)
            ln_stats(0)
            pool_difference(2)
            unit_lo(7)
            pool_difference(1)
            ya_lo(0)
            pool_difference(0)
            for n in range(GROUPS):
                difference_lo(n)
            unit_lo(8)
            unit_lo(9)
            yb_lo(0)
            yb_lo(1)
            conv_taps((1, 1, 8))
            yb_lo(2)
            yb_lo(3)
            conv_taps((1, 1, 11), (2, 1, 8))
            x1(0)
            conv_taps((2, 1, 3))
            norm_apply(FFN, 0, 2)
            conv_taps((2, 1, 8), (3, 1, 2))
            x1(1)
            conv_taps((3, 1, 4))
            norm_apply(FFN, 1, 2)
            t2_lo(0)
            conv_taps((3, 1, 12))
            x1(2)
            t2_lo(1)
            norm_apply(FFN, 2, 2)
            ln_stats(1)
            ya_lo(1)

            def ffn_lo(kind, i, t, par):
                s = FFN_SLOT[kind]
                dve.wait_ge(hi_done, ffn_half(kind, i, t) + HI0)
                nc.vector.tensor_tensor(half_of(w_lo[s][:, :], kind != "d", t),
                                        half_of(raw[:, par, :], kind != "d", t),
                                        half_of(w_hi[s][:, :].bitcast(F32), kind != "d", t),
                                        ALU.subtract).then_inc(lo_done, 1)

            for m in range(HT - 1, TT):
                x1(m)
                norm_apply(FFN, m, 2)
                t2_lo(m - 1)
                if m == TT - 2:
                    ffn_lo("g", 0, 0, 0)
                    ffn_lo("v", 0, 0, 1)
            t2_lo(TT - 1)
            ffn_lo("g", 0, 1, 0)
            ffn_lo("v", 0, 1, 1)

            def gate(i, t):
                f = i * 2 + t
                c = fchan[:, f, :] if isinstance(i, int) else fchan[:, bass.ds(f, 1), :].squeeze(1)
                ps = slot[(F_SLOT + 2 * t) % 4]
                dve.wait_ge(last_tap_done, i * 2 + (t + 1))
                for s in (1, 2):
                    if s == 2:
                        dve.wait_ge(gate_one, i * 2 + (t + 1))
                    nc.vector.scalar_tensor_tensor(tmp[:, t, s:SEQ], ps[:, 0:SEQ - s],
                                                   c[:, FTAPS - 1 - s:FTAPS - s], tmp[:, t, s:SEQ],
                                                   ALU.mult, ALU.add).then_inc(gate_one if s == 1 else gate_taps, 1)

            def gate_times_value(i, t):
                dve.wait_ge(gate_silu, i * 2 + (t + 1))
                dve.wait_ge(pe_done, up_job(i, 2 * t + 1) + 1)
                nc.vector.tensor_tensor(tmp[:, t, :], tmp[:, t, :], slot[(F_SLOT + 2 * t + 1) % 4][:, :],
                                        ALU.mult).then_inc(gated, 1)

            def gv_low(i, t, par):
                dve.wait_ge(gv_hi_done, i * 2 + (t + 1))
                nc.vector.tensor_tensor(gv_lo[:, par, t, :], tmp[:, t, :], gv_hi[:, par, t, :].bitcast(F32),
                                        ALU.subtract).then_inc(gv_lo_done, 1)

            def add_down(i, m):
                dve.wait_ge(pe_done, down_job(i, m) + 1)
                if isinstance(i, int) and i == 0:
                    dve.wait_ge(normed, 2 * TT)
                else:
                    dve.wait_ge(x_added, i * TT + (m - TT + 1))
                last = isinstance(i, int) and i == CHUNKS - 1
                nc.vector.tensor_tensor(x_sb[:, m, :], x_sb[:, m, :], slot[(F_SLOT + m) % 4][:, :],
                                        ALU.add).then_inc(x2_done if last else x_added, 1)

            def body(i, par, down=True, last=False):
                gpar, vpar = (par, 1 - par) if down else (0, 1)
                if down:
                    ffn_lo("d", i - 1, 0, 1 - par)
                    ffn_lo("d", i - 1, 1, 1 - par)
                gate(i, 0)
                if not last:
                    ffn_lo("g", i + 1, 0, gpar)
                gate_times_value(i, 0)
                if not last:
                    ffn_lo("v", i + 1, 0, vpar)
                gv_low(i, 0, par)
                gate(i, 1)
                if not last:
                    ffn_lo("g", i + 1, 1, gpar)
                gate_times_value(i, 1)
                if not last:
                    ffn_lo("v", i + 1, 1, vpar)
                if down:
                    add_down(i - 1, 0)
                gv_low(i, 1, par)
                if down:
                    for m in range(1, TT):
                        add_down(i - 1, m)

            body(0, 0, down=False)
            body(1, 1)
            body(2, 0)
            with dve.Fori(3, CHUNKS - 2, 2) as i:
                body(i, 1)
                body(i + 1, 0)
            body(CHUNKS - 2, 1)
            body(CHUNKS - 1, 0, last=True)
            for t in range(2):
                ffn_lo("d", CHUNKS - 1, t, 0)
            dve.wait_ge(lo_done, LO0 + ffn_half("d", CHUNKS - 1, 1))
            for m in range(TT):
                add_down(CHUNKS - 1, m)
                if m >= 1:
                    norm_apply(FINAL, m - 1, 3)
            norm_apply(FINAL, TT - 1, 3)

        @block.tensor
        def _(pe):
            last_in = {}

            def slot_read(n):
                if SLOT[n] in last_in:
                    pe.wait_ge(*read[last_in[SLOT[n]]])
                last_in[SLOT[n]] = n

            def three_passes(out_ap, st, mv, first, last):
                for s, v in ((0, 0), (0, 1), (1, 0)):
                    mm = nc.tensor.matmul(out_ap, st[s], mv[v], start=first and s == v == 0,
                                          stop=last and s == 1)
                return mm

            act = (act_hi, act_lo)
            bank = [slice(0, BANK), slice(BANK, 2 * BANK)]

            def constants():
                pe.wait_ge(consts_loaded, 16 * 7)
                slot_read(J_CONST)
                ps = slot_of(J_CONST)
                for c in range(CT):
                    nc.tensor.transpose(ps[:, c * ROWS:(c + 1) * ROWS], raw_rows[0:ROWS, c * P:(c + 1) * P],
                                        ident[0:ROWS, 0:ROWS])
                R = FTAPS + 1
                for c in range(FT):
                    mm = nc.tensor.transpose(ps[:, BANK + c * R:BANK + (c + 1) * R],
                                             raw_frows[0:R, c * P:(c + 1) * P], ident[0:R, 0:R])
                mm.then_inc(pe_done, 1)

            def transpose_tile(n, m, count):
                slot_read(n)
                pe.wait_ge(normed, count)
                for k in range(KT):
                    mm = nc.tensor.transpose(slot_of(n)[:, k * P:(k + 1) * P], tmp[:, m % 2, k * P:(k + 1) * P],
                                             ident[:, :])
                mm.then_inc(pe_done, 1)

            pe.wait_ge(ident_ready, 2)
            for m in range(HT + 1):
                if m == 3:
                    constants()
                transpose_tile(J_T1[m], m, m + 1)

            def column_part(ps, s, t, h):
                w = [whole(b[s][:, :], True)[:, :, t * P:(t + 1) * P] for b in (w_hi, w_lo)]
                for k in range(KT):
                    mm = three_passes(ps[:, bank[h]], [b[:, k, :] for b in w],
                                      [a[:, k, bank[h]] for a in act], k == 0, k == KT - 1)
                return mm

            def column_tile(ps, s, t):
                column_part(ps, s, t, 0)
                column_part(ps, s, t, 1).then_inc(pe_done, 1)

            order = [(2 * (j // 2) + b, j % 2) for j in range(CT) for b in range(2)] + [(4, 1), (4, 0), (5, 1), (5, 0)]

            def in_projection(n):
                q, t = order[n]
                slot_read(J_IN[n])
                pe.wait_ge(lo_done, 2 * (q - POOL_UNITS) + t + 1)
                column_tile(slot_of(J_IN[n]), W_SLOT[q], t)

            for n in range(2):
                slot_read(J_IN[n])
                pe.wait_ge(lo_pool_done, 2 * n + 1)
                pe.wait_ge(act_lo_done, DONE["t1", HT - 1])
                column_part(slot_of(J_IN[n]), W_SLOT[n], 0, 0)
                for m in ((5, 6), (7,))[n]:
                    transpose_tile(J_T1[m], m, m + 1)
            pe.wait_ge(act_lo_done, DONE["t1", TT - 1])
            for n in range(2):
                column_part(slot_of(J_IN[n]), W_SLOT[n], 0, 1).then_inc(pe_done, 1)
            for n in range(2):
                pe.wait_ge(lo_pool_done, 2 * n + 2)
                slot_read(J_IN[2 + n])
                column_tile(slot_of(J_IN[2 + n]), W_SLOT[n], 1)

            def ln_to_tokens(h):
                pe.wait_ge(conv_done[h], CT)
                for b in range(2):
                    n = J_LN[h][b]
                    slot_read(n)
                    for i in range(2):
                        for j in range(CT):
                            cols = slice((2 * b + i) * P, (2 * b + i + 1) * P)
                            mm = nc.tensor.transpose(slot_of(n)[:, i * BANK + j * P:i * BANK + (j + 1) * P],
                                                     conv[:, h, j, cols], ident[:, :])
                    mm.then_inc(pe_done, 1)

            def ln_back(h):
                pe.wait_ge(z_done, HT * (h + 1))
                for b in range(2):
                    n = J_BACK[h][b]
                    slot_read(n)
                    for jj in range(2):
                        for i in range(HT):
                            at = (i % 2) * BANK + (2 * b + jj) * P
                            mm = nc.tensor.transpose(slot_of(n)[:, jj * BANK + i * P:jj * BANK + (i + 1) * P],
                                                     z_sb[:, i // 2, at:at + P], ident[:, :])
                    mm.then_inc(pe_done, 1)

            def out_unit(m, r):
                n = J_OUT[m]
                if r == 0:
                    slot_read(n)
                    pe.wait_ge(act_lo_done, DONE["ya", m // HT, CT - 1])
                if r == 2:
                    pe.wait_ge(act_lo_done, DONE["yb", GROUPS - 1])
                cols = slice(m * P, (m + 1) * P)
                q, k0, last = U_OUT + r, OUT_ROWS[r], r == len(OUT_ROWS) - 1
                pe.wait_ge(lo_done, 2 * (q - POOL_UNITS) + 2)
                for kk in range(2):
                    for h in range(2):
                        mm = three_passes(slot_of(n)[:, bank[h]], [a[:, k0 + kk, cols] for a in act],
                                          [whole(b[W_SLOT[q]][:, :], False)[:, kk, bank[h]] for b in (w_hi, w_lo)],
                                          r == kk == 0, last and kk == 1)
                if last:
                    mm.then_inc(pe_done, 1)
                elif m == TT - 1 and r < 2:
                    mm.then_inc(out_used, 1)

            def out_projection(m):
                for r in range(len(OUT_ROWS)):
                    out_unit(m, r)

            def t2(m):
                transpose_tile(J_T2[m], m, TT + m + 1)

            for n in range(4, 2 * CT + 3):
                in_projection(n)
            ln_to_tokens(0)
            q, t = order[-1]
            slot_read(J_IN[-1])
            pe.wait_ge(lo_done, 2 * (q - POOL_UNITS) + t + 1)
            column_part(slot_of(J_IN[-1]), W_SLOT[q], t, 0)
            ln_back(0)
            column_part(slot_of(J_IN[-1]), W_SLOT[q], t, 1).then_inc(pe_done, 1)

            def pool_product(n):
                g = GROUPS - 1 - n
                slot_read(J_POOL[n])
                pe.wait_ge(act_lo_done, DONE["diff", n])
                for h in range(2):
                    mm = three_passes(slot_of(J_POOL[n])[:, bank[h]], (pw_hi[:, g, :], pw_lo[:, g, :]),
                                      [a[:, CT + g, bank[h]] for a in act], True, True)
                mm.then_inc(pe_done, 1)

            out_unit(0, 0)
            out_unit(0, 1)
            pe.wait_ge(pw_done, 2)
            pool_product(0)
            pool_product(1)
            out_unit(1, 0)
            pool_product(2)
            pool_product(3)
            out_unit(1, 1)
            for m in range(2):
                out_unit(m, 2)
                out_unit(m, 3)
            t2(0)
            out_projection(2)
            t2(1)
            ln_to_tokens(1)
            out_unit(3, 0)
            out_unit(3, 1)
            ln_back(1)
            out_unit(3, 2)
            out_unit(3, 3)
            for m in range(HT, TT):
                t2(m - 2)
                out_projection(m)

            def up(i, t, kind, first=False):
                r = 2 * t + (kind == "v")
                if first:
                    slot_read(J_FFN + r)
                elif isinstance(i, int) and i == 1:
                    pe.wait_ge(gate_taps if kind == "g" else gated, t + 1)
                else:
                    pe.wait_ge(x_added, i * TT + (r + UPS - 2 * TT + 1))
                pe.wait_ge(lo_done, ffn_half(kind, i, t) + LO0)
                column_tile(slot[(F_SLOT + r) % 4], FFN_SLOT[kind], t)

            def down(i, par):
                last = isinstance(i, int) and i == CHUNKS - 1
                for m in range(TT):
                    if m < UPS:
                        if last:
                            pe.wait_ge(x_added, i * TT + (m - UPS + 1))
                        else:
                            pe.wait_ge(gated if m % 2 else gate_taps, i * 2 + (2 + m // 2 + 1))
                    else:
                        pe.wait_ge(x2_done if last else x_added, (0 if last else i * TT) + (m - UPS + 1))
                    if m == 0:
                        pe.wait_ge(lo_done, ffn_half("d", i, 1) + LO0)
                        pe.wait_ge(gv_lo_done, i * 2 + 2)
                    cols = slice(m * P, (m + 1) * P)
                    for kk in range(2):
                        for h in range(2):
                            mm = three_passes(slot[(F_SLOT + m) % 4][:, bank[h]],
                                              [b[:, par, kk, cols] for b in (gv_hi, gv_lo)],
                                              [whole(b[FFN_SLOT["d"]][:, :], False)[:, kk, bank[h]]
                                               for b in (w_hi, w_lo)], kk == 0, kk == 1)
                    mm.then_inc(pe_done, 1)

            def body(i, par):
                for t in range(2):
                    up(i, t, "g")
                    up(i, t, "v")
                down(i - 1, 1 - par)

            pe.wait_ge(act_lo_done, DONE["t2", HT - 1])
            for r, kind in enumerate("gv"):
                slot_read(J_FFN + r)
                pe.wait_ge(lo_done, LO0 + ffn_half(kind, 0, 0))
                column_part(slot_of(J_FFN + r), FFN_SLOT[kind], 0, 0)
                t2(TT - 2 + r)
            pe.wait_ge(act_lo_done, DONE["t2", TT - 1])
            for r, kind in enumerate("gv"):
                column_part(slot_of(J_FFN + r), FFN_SLOT[kind], 0, 1).then_inc(pe_done, 1)
            up(0, 1, "g", first=True)
            up(0, 1, "v", first=True)
            body(1, 1)
            body(2, 0)
            with pe.Fori(3, CHUNKS - 2, 2) as i:
                body(i, 1)
                body(i + 1, 0)
            body(CHUNKS - 2, 1)
            body(CHUNKS - 1, 0)
            down(CHUNKS - 1, 0)


_INS = ["x", "norm_mix_g", "w_in", "conv_a_w", "conv_a_b", "ln_a_g", "ln_a_b", "pool_w", "pool_scale",
        "w_out", "norm_ffn_g", "w_up", "conv_f_w", "conv_f_b", "w_down", "norm_final_g"]


def kernel(**inputs):
    import numpy as np
    import concourse.bacc as bacc
    from concourse.bass_utils import run_bass_kernel_spmd

    nc = bacc.Bacc("TRN2", target_bir_lowering=False, num_devices=1,
                   dynamic_dma_scratch_size=1024)
    arrays, args = {}, []
    for name in _INS:
        a = np.ascontiguousarray(inputs[name])
        arrays[f"in_{name}"] = a
        args.append(nc.dram_tensor(f"in_{name}", a.shape, mybir.dt.from_np(a.dtype), kind="ExternalInput").ap())
    out = nc.dram_tensor("out_0", inputs["x"].shape, F32, kind="ExternalOutput").ap()
    hybrid_block(nc, *args, out)
    result = run_bass_kernel_spmd(nc, [arrays], core_ids=[0])
    return result.results[0]["out_0"]
```

```python
from contextlib import ExitStack

import concourse.bass as bass
from concourse import mybir

P = 128
BANK = 512
F32 = mybir.dt.float32
F32R = mybir.dt.float32r
ALU = mybir.AluOpType
ACT = mybir.ActivationFunctionType


def hybrid_block(nc, x, norm_mix_g, w_in, conv_a_w, conv_a_b, ln_a_g, ln_a_b, pool_w, pool_scale,
                 w_out, norm_ffn_g, w_up, conv_f_w, conv_f_b, w_down, norm_final_g, out):
    _, SEQ, D = x.shape
    DEPTH, TAPS, D_CONV = conv_a_w.shape
    GROUPS, GDIM = pool_w.shape[1:3]
    D_FF = w_down.shape[1]
    FTAPS = conv_f_w.shape[1]
    WINDOWS = (2, 4, 8, 16)
    EPS = 1e-6
    KT = D // P
    TT = SEQ // P
    HALF = SEQ // 2
    HT = TT // 2
    CT = D_CONV // P
    FT = D_FF // P
    CHUNKS = FT // 2
    W2 = 2 * P
    assert DEPTH == 1 and SEQ == D == 2 * BANK and GDIM == P and GROUPS == CT == 4
    assert FT == 2 * CHUNKS and CHUNKS % 2 == 1 and FTAPS == 3 and KT == TT == 8

    x_rows = x.rearrange("b (m p) d -> p (b m) d", p=P)
    out_rows = out.rearrange("b (m p) d -> p (b m) d", p=P)
    w_in_v = w_in[0].rearrange("(k p) n -> p k n", p=P)
    w_out_v = w_out[0].rearrange("(k p) n -> p k n", p=P)
    w_up_v = w_up[0].rearrange("(k p) n -> p k n", p=P)
    w_down_v = w_down[0].rearrange("(k p) n -> p k n", p=P)
    pool_w_v = pool_w[0].rearrange("g c d -> c g d")

    counter = [0]

    def jobs(n):
        counter[0] += n
        return list(range(counter[0] - n, counter[0]))

    SLOT, J = {}, {}
    for key, s in (
            [(("t1", 0), 3), (("t1", 1), 2), (("t1", 2), 1), (("t1", 3), 0), (("t1", 4), 2),
             (("t1", 5), 3), (("t1", 6), 0), (("t1", 7), 3), (("const",), 0)] +
            [(("in", n), (n + 1) % 4) for n in range(2 * CT + 3)] +
            [(("ln", 0, 0), 0), (("ln", 0, 1), 1), (("back", 0, 0), 3), (("back", 0, 1), 0), (("in", 2 * CT + 3), 2)] +
            [(("pool", 0), 3), (("pool", 1), 0), (("pool", 2), 3), (("pool", 3), 0)] +
            [(("out", 0), 1), (("out", 1), 2), (("out", 2), 0), (("t2", 0), 3), (("t2", 1), 1),
             (("ln", 1, 0), 3), (("ln", 1, 1), 0), (("out", 3), 2), (("back", 1, 0), 3), (("back", 1, 1), 0),
             (("out", 4), 1), (("t2", 2), 3), (("t2", 3), 0), (("out", 5), 2), (("t2", 4), 1),
             (("out", 6), 3), (("t2", 5), 2), (("out", 7), 0), (("t2", 6), 3), (("t2", 7), 0)]):
        J[key] = jobs(1)[0]
        SLOT[J[key]] = s
    J_CONST = J["const",]
    J_T1, J_OUT, J_T2 = ([J[kind, m] for m in range(TT)] for kind in ("t1", "out", "t2"))
    J_IN = [J["in", n] for n in range(2 * CT + GROUPS)]
    J_POOL = [J["pool", n] for n in range(GROUPS)]
    J_LN, J_BACK = ([[J[kind, h, b] for b in range(2)] for h in range(2)] for kind in ("ln", "back"))
    F_SLOT = 1
    UPS = 4
    J_FFN = jobs(UPS)[0]
    J_BODY = counter[0]
    BODY = UPS + TT
    SLOT |= {J_FFN + n: (F_SLOT + n) % 4 for n in range(UPS)}

    def up_job(i, r):
        return J_FFN + r if isinstance(i, int) and i == 0 else i * BODY + (J_BODY - BODY + r)

    def down_job(i, m):
        if isinstance(i, int) and i == CHUNKS - 1:
            return J_BODY + i * BODY + m
        return i * BODY + (J_BODY + UPS + m)

    IN_COLS = (0, D_CONV, W2, D_CONV + W2, 2 * D_CONV + W2, 2 * D_CONV)
    OUT_ROWS = (0, 2, 6, 4)
    U_OUT = len(IN_COLS)
    U_FFN = U_OUT + len(OUT_ROWS)
    W_SLOT = (0, 1, 2, 0, 1, 2, 0, 1, 2, 3)

    def ffn_slot(kind, i):
        return 0 if isinstance(i, int) and i == CHUNKS - 1 and kind == "d" else "gvd".index(kind)

    POOL_UNITS = 3

    def half_count(q, t):
        return 2 * t + q + 1 if q < 2 else 2 * q + t + 1

    HI0, LO0 = 2 * U_FFN, 2 * (U_FFN - POOL_UNITS)

    def ffn_half(kind, i, t):
        if kind == "d":
            return 6 * (CHUNKS - 1) + 5 + t if isinstance(i, int) and i == CHUNKS - 1 else i * 6 + (9 + t)
        o = 2 * t + (kind == "v")
        return 1 + o if isinstance(i, int) and i == 0 else i * 6 + (o - 1)

    def raw_loads(q, par):
        return q * 8 + (16 - 8 * par)

    with ExitStack() as ctx:
        def sb(name, shape, dt=F32):
            return ctx.enter_context(nc.sbuf_tensor(name, shape, dt))

        def sem(name):
            return ctx.enter_context(nc.semaphore(name))

        ROWS = TAPS + 4
        BIAS, LN_G, LN_B, SCALE = range(TAPS, ROWS)
        x_sb = sb("x_sb", [P, TT, D])
        act_hi = sb("act_hi", [P, KT, SEQ], F32R)
        act_lo = sb("act_lo", [P, KT, SEQ], F32R)
        raw = sb("raw", [P, 2, 2 * D])
        w_hi = [sb(f"w_hi{s}", [P, 2 * D], F32R) for s in range(3)]
        w_lo = [sb(f"w_lo{s}", [P, 2 * D], F32R) for s in range(3)]
        tmp = sb("tmp", [P, 2, SEQ])
        z_sb = sb("z_sb", [P, 2, SEQ])
        RING = 4
        prod = sb("prod", [P, RING, HALF])
        ident = sb("ident", [P, P])
        chan = sb("chan", [P, CT, ROWS])
        fchan = sb("fchan", [P, FT, FTAPS + 1])
        inv_count = sb("inv_count", [P, WINDOWS[-1]])
        edge = sb("edge", [P, WINDOWS[-1]])
        eps = sb("eps", [P, 1])
        warm = sb("warm", [P, 1])
        IN, FFN, FINAL, LN = range(4)
        sumsq = sb("sumsq", [P, 3, TT])
        std = sb("std", [P, 4, TT])
        rstd = sb("rstd", [P, 4, TT])
        bn = sb("bn", [P, TT, 6])
        mean_var = sb("mean_var", [P, TT, 2])
        shift = sb("shift", [P, TT])
        with nc.sbuf_tensor("pw_hi", [P, GROUPS, P], F32R) as pw_hi:
            with nc.sbuf_tensor("pw_lo", [P, GROUPS, P], F32R) as pw_lo:
                pass
        gain = sb("gain", [P, D])
        with nc.sbuf_tensor("conv", [P, 2, CT, HALF], F32) as conv:
            with nc.sbuf_tensor("tokens", [P, GROUPS, SEQ], F32) as tokens:
                pass
            with nc.sbuf_tensor("w_hi3", [P, 2 * D], F32R) as w_hi3:
                with nc.sbuf_tensor("w_lo3", [P, 2 * D], F32R) as w_lo3:
                    pass
        gv_hi = sb("gv_hi", [P, 2, 2, SEQ], F32R)
        gv_lo = sb("gv_lo", [P, 2, 2, SEQ], F32R)
        w_hi.append(w_hi3)
        w_lo.append(w_lo3)
        raw_rows = conv[:, 0, 0, :]
        raw_frows = tokens[:, :, :].rearrange("p a b -> p (a b)")[:, 0:D_FF]
        pw_raw = conv[:, 1, 0, :].rearrange("p (g d) -> p g d", g=GROUPS)
        u = x_sb[:, HT:TT, :]

        slot = [ctx.enter_context(nc.psum_tensor(f"slot{s}", [P, 2 * BANK], F32)) for s in range(4)]

        def slot_of(n):
            return slot[SLOT[n]]

        consts_loaded = sem("consts_loaded")
        pool_w_loaded = sem("pool_w_loaded")
        gain_loaded = sem("gain_loaded")
        x_loaded = [sem(f"x_loaded{m}") for m in range(TT)]
        raw_loaded = [sem(f"raw_loaded{b}") for b in range(2)]
        stored = [sem(f"stored{b}") for b in range(4)]
        ident_ready = sem("ident_ready")
        small_ready = sem("small_ready")
        pe_done = sem("pe_done")
        chan_ready = sem("chan_ready")
        hi_done = sem("hi_done")
        lo_done = sem("lo_done")
        lo_pool_done = sem("lo_pool_done")
        pw_done = sem("pw_done")
        squares_done = sem("squares_done")
        std_done = sem("std_done")
        rstd_done = sem("rstd_done")
        normed = sem("normed")
        act_hi_done = sem("act_hi_done")
        act_lo_done = sem("act_lo_done")
        gate_half_done = sem("gate_half_done")
        sig_half_done = sem("sig_half_done")
        u_half_done = sem("u_half_done")
        sig_done = sem("sig_done")
        u_done = sem("u_done")
        first_tap_done = sem("first_tap_done")
        product_done = sem("product_done")
        light_step = sem("light_step")
        conv_step = sem("conv_step")
        conv_done = [sem(f"conv_done{h}") for h in range(2)]
        out_used = sem("out_used")
        tokens_ready = sem("tokens_ready")
        window_step = sem("window_step")
        d_step = sem("d_step")
        ln_step = sem("ln_step")
        ln_std_done = sem("ln_std_done")
        z_done = sem("z_done")
        silu_done = sem("silu_done")
        x1_done = sem("x1_done")
        last_tap_done = sem("last_tap_done")
        gate_one = sem("gate_one")
        gate_taps = sem("gate_taps")
        gate_silu = sem("gate_silu")
        gated = sem("gated")
        gv_hi_done = sem("gv_hi_done")
        gv_lo_done = sem("gv_lo_done")
        x_added = sem("x_added")
        x2_done = sem("x2_done")
        out_ready = sem("out_ready")

        PIECES = ([("t1", m) for m in range(TT)] + [("ya", 0, j) for j in range(CT)] +
                  [("diff", 0), ("diff", 1), ("diff", 2), ("yb", 0), ("yb", 1), ("diff", 3), ("yb", 2), ("yb", 3)] +
                  [("t2", m) for m in range(HT - 2)] + [("ya", 1, j) for j in range(CT)] +
                  [("t2", m) for m in range(HT - 2, TT)])
        DONE = {piece: n + 1 for n, piece in enumerate(PIECES)}

        LIGHT = {(0, 1): 17, (1, 0): 15, (2, 0): 16, (3, 0): 15, (2, 1): 17, (3, 1): 17}
        APART = CT - 1
        light_before, light_first = {}, {}
        for jh in LIGHT:
            light_first[jh] = len(light_first)
            light_before[jh] = sum(LIGHT[b] - 1 for b in light_before)

        WINDOW_STEPS = [sum(2 * (k + 1) for k in range(g, GROUPS)) for g in range(GROUPS)]
        LN_STEPS = 2 * HT + 2

        read = {J_CONST: (chan_ready, 2)}
        read |= {J_T1[m]: (act_lo_done, DONE["t1", m]) for m in range(TT)}
        for j in range(CT):
            read[J_IN[2 * j]] = (u_done, j + 1)
            read[J_IN[2 * j + 1]] = (sig_done, j + 1)
            read[J_IN[2 * CT + j]] = (tokens_ready, j + 1)
            read[J_POOL[j]] = (act_lo_done, DONE["yb", j])
        for h in range(2):
            for b in range(2):
                read[J_LN[h][b]] = (z_done, HT * h + 2 * b + 2)
                read[J_BACK[h][b]] = (act_lo_done, DONE["ya", h, 2 * b + 1])
        for m in range(TT):
            read[J_OUT[m]] = (x1_done, m + 1)
            read[J_T2[m]] = (act_lo_done, DONE["t2", m])

        def half_of(buf, columns, t):
            if columns:
                return buf.rearrange("p (k n) -> p k n", k=KT)[:, :, t * P:(t + 1) * P]
            return buf[:, t * D:(t + 1) * D]

        def whole(buf, columns):
            return buf.rearrange("p (k n) -> p k n", k=KT if columns else 2)

        block = ctx.enter_context(nc.Block())

        @block.sync
        def _(sp):
            def load_x(m):
                sp.dma_start(x_sb[:, m, :], x_rows[:, m, :]).then_inc(x_loaded[m], 16)

            def load_gain(src):
                sp.dma_start(gain[:, :], src.broadcast_to([P, D])).then_inc(gain_loaded, 16)

            def load_unit(q):
                if q >= 2 + POOL_UNITS:
                    sp.wait_ge(lo_done, 2 * (q - 2 - POOL_UNITS) + 2)
                elif q >= 2:
                    sp.wait_ge(lo_pool_done, half_count(q - 2, 1))
                if q < U_OUT:
                    src = w_in_v[:, :, IN_COLS[q]:IN_COLS[q] + W2]
                else:
                    src = w_out_v[:, OUT_ROWS[q - U_OUT]:OUT_ROWS[q - U_OUT] + 2, :]
                sp.dma_start(whole(raw[:, q % 2, :], q < U_OUT), src).then_inc(raw_loaded[q % 2], 16)

            def load_ffn(kind, i, par):
                if kind == "d":
                    src = w_down_v[:, bass.ds(i * 2, 2), :]
                else:
                    src = w_up_v[:, :, bass.ds(i * W2 + (D_FF if kind == "v" else 0), W2)]
                sp.dma_start(whole(raw[:, par, :], kind != "d"), src).then_inc(raw_loaded[par], 16)

            load_x(0)
            load_gain(norm_mix_g)
            for m in range(1, HT):
                load_x(m)
            load_unit(0)
            load_unit(1)
            for m in range(HT, TT):
                load_x(m)
            sp.dma_start(raw_rows[0:TAPS, :], conv_a_w[0]).then_inc(consts_loaded, 16)
            for r, v in ((BIAS, conv_a_b), (LN_G, ln_a_g), (LN_B, ln_a_b), (SCALE, pool_scale)):
                sp.dma_start(raw_rows[r:r + 1, :], v).then_inc(consts_loaded, 16)
            sp.dma_start(raw_frows[0:FTAPS, :], conv_f_w[0]).then_inc(consts_loaded, 16)
            sp.dma_start(raw_frows[FTAPS:FTAPS + 1, :], conv_f_b).then_inc(consts_loaded, 16)
            sp.dma_start(pw_raw, pool_w_v).then_inc(pool_w_loaded, 16)
            for q in range(2, U_FFN):
                load_unit(q)
            sp.wait_ge(pe_done, J_POOL[-1] + 1)
            load_gain(norm_ffn_g)
            sp.wait_ge(lo_done, LO0 - 2)
            load_ffn("g", 0, 0)
            sp.wait_ge(lo_done, LO0)
            load_ffn("v", 0, 1)
            for j in range(CT):
                for h in range(2):
                    sp.wait_ge(conv_done[h], j + 1)
                load_x(HT + j)
            sp.wait_ge(lo_done, LO0 + ffn_half("g", 0, 1))
            load_ffn("g", 1, 0)
            sp.wait_ge(lo_done, LO0 + ffn_half("v", 0, 1))
            load_ffn("v", 1, 1)

            def body(i, par, last=False):
                sp.wait_ge(lo_done, ffn_half("g", i, 1) + LO0)
                load_ffn("d", i - 1, par)
                if not last:
                    sp.wait_ge(lo_done, ffn_half("v", i, 1) + LO0)
                    load_ffn("g", i + 1, 1 - par)
                    sp.wait_ge(lo_done, ffn_half("d", i - 1, 1) + LO0)
                    load_ffn("v", i + 1, par)

            with sp.Fori(1, CHUNKS - 2, 2) as i:
                body(i, 0)
                body(i + 1, 1)
            body(CHUNKS - 2, 0)
            body(CHUNKS - 1, 1, last=True)
            sp.wait_ge(lo_done, LO0 + ffn_half("v", CHUNKS - 1, 1))
            load_ffn("d", CHUNKS - 1, 0)
            sp.wait_ge(normed, 2 * TT)
            load_gain(norm_final_g.rearrange("(a d) -> a d", a=1))
            for m in range(TT):
                sp.wait_ge(out_ready, m + 1)
                sp.dma_start(out_rows[:, m, :], raw[:, m % 4 // 2, (m % 2) * D:(m % 2 + 1) * D])\
                  .then_inc(stored[m % 4], 16)
            for b in range(4):
                sp.wait_ge(stored[b], 16 * TT // 4)

        @block.gpsimd
        def _(pool):
            nc.gpsimd.memset(ident[:, :], 0.0).then_inc(ident_ready, 1)
            pool.wait_ge(ident_ready, 1)
            nc.gpsimd.affine_select(out=ident[:, :], in_=ident[:, :], compare_op=ALU.not_equal, fill=1.0,
                                    base=0, pattern=[[-1, P]], channel_multiplier=1).then_inc(ident_ready, 1)
            nc.gpsimd.memset(eps[:, :], EPS).then_inc(small_ready, 1)
            for t in range(WINDOWS[-1]):
                nc.gpsimd.memset(inv_count[:, t:t + 1], 1.0 / (t + 1)).then_inc(small_ready, 1)

            def half_lo(q, t):
                s = W_SLOT[q]
                pool.wait_ge(hi_done, half_count(q, t))
                nc.gpsimd.tensor_tensor(half_of(w_lo[s][:, :], True, t), half_of(raw[:, q % 2, :], True, t),
                                        half_of(w_hi[s][:, :].bitcast(F32), True, t),
                                        ALU.subtract).then_inc(lo_pool_done, 1)

            def windows(g, before):
                pool.wait_ge(tokens_ready, GROUPS - g)
                if g == GROUPS - 1:
                    pool.wait_ge(u_done, CT)
                else:
                    pool.wait_ge(d_step, 3 * (GROUPS - 1 - g))
                src = tokens[:, g, :]
                for b in range(g + 1):
                    w, dst = 2 ** b, tmp[:, b % 2, :]
                    if b:
                        pool.wait_ge(window_step, before + 2 * b)
                    nc.gpsimd.tensor_tensor(dst[:, w:SEQ], src[:, w:SEQ], src[:, 0:SEQ - w],
                                            ALU.add).then_inc(window_step, 1)
                    nc.gpsimd.tensor_copy(dst[:, 0:w], src[:, 0:w]).then_inc(window_step, 1)
                    src = dst

            def light_taps(j, h, first=1, end=TAPS):
                pool.wait_ge(first_tap_done, light_first[j, h] + 1)
                for s in range(first, min(end, LIGHT[j, h])):
                    n = light_before[j, h] + s - 1
                    pool.wait_ge(product_done, n + 1)
                    if s > 1:
                        pool.wait_ge(light_step, n)
                    dst = conv[:, h, j, (s if h == 0 else 0):HALF]
                    nc.gpsimd.tensor_tensor(dst, dst, prod[:, n % RING, (s if h == 0 else 0):HALF],
                                            ALU.add).then_inc(light_step, 1)

            for t in range(2):
                for q in range(2):
                    half_lo(q, t)
            pool.wait_ge(pw_done, 1)
            nc.gpsimd.tensor_tensor(pw_lo[:, :, :], pw_raw, pw_hi[:, :, :].bitcast(F32),
                                    ALU.subtract).then_inc(pw_done, 1)
            half_lo(2, 0)
            half_lo(2, 1)
            light_taps(0, 1)
            light_taps(1, 0)
            light_taps(2, 0)
            light_taps(3, 0)
            windows(3, 0)
            light_taps(2, 1, 1, 3)
            windows(2, WINDOW_STEPS[3])
            light_taps(2, 1, 3, 4)
            windows(1, WINDOW_STEPS[2])
            light_taps(2, 1, 4, 5)
            windows(0, WINDOW_STEPS[1])
            light_taps(2, 1, 5)
            light_taps(3, 1)

        @block.scalar
        def _(act):
            def norm_std(row, m):
                n = row * TT + m + 1
                act.wait_ge(squares_done, n - 1)
                squares = (z_sb if row == IN else tmp)[:, m % 2, :]
                nc.scalar.activation(squares, x_sb[:, m, :], ACT.Square,
                                     accum_out=sumsq[:, row, m:m + 1]).then_inc(squares_done, 1)
                act.wait_ge(squares_done, n)
                nc.scalar.activation(std[:, row, m:m + 1], sumsq[:, row, m:m + 1], ACT.Sqrt,
                                     bias=eps[:, 0:1], scale=1.0 / D).then_inc(std_done, 1)

            def transposed_hi(n, m):
                act.wait_ge(pe_done, n + 1)
                nc.scalar.activation(act_hi[:, :, m * P:(m + 1) * P],
                                     slot_of(n)[:, :].rearrange("p (k n) -> p k n", k=KT),
                                     ACT.Copy).then_inc(act_hi_done, 1)

            def half_hi(q, t):
                s, columns = W_SLOT[q], q < U_OUT
                nc.scalar.activation(half_of(w_hi[s][:, :], columns, t),
                                     half_of(raw[:, q % 2, :], columns, t), ACT.Copy).then_inc(hi_done, 1)

            def unit_hi(q, last_user=None):
                act.wait_ge(raw_loaded[q % 2], raw_loads(q, q % 2))
                if last_user is not None:
                    act.wait_ge(pe_done, last_user + 1)
                for t in range(2):
                    half_hi(q, t)

            act.wait_ge(small_ready, 1)
            nc.scalar.activation(warm[:, :], eps[:, :], ACT.Sqrt)
            for m in range(TT):
                act.wait_ge(x_loaded[m], 16)
                norm_std(IN, m)
                if m >= 1:
                    transposed_hi(J_T1[m - 1], m - 1)
                if 2 <= m < 6:
                    act.wait_ge(raw_loaded[m % 2], 16)
                    half_hi(m % 2, m // 2 - 1)
            transposed_hi(J_T1[TT - 1], TT - 1)
            act.wait_ge(pe_done, J_CONST + 1)
            consts = slot_of(J_CONST)
            nc.scalar.activation(chan[:, :, :], consts[:, 0:CT * ROWS]
                                 .rearrange("p (c r) -> p c r", c=CT), ACT.Copy).then_inc(chan_ready, 1)
            nc.scalar.activation(fchan[:, :, :], consts[:, BANK:BANK + FT * (FTAPS + 1)]
                                 .rearrange("p (c r) -> p c r", c=FT), ACT.Copy).then_inc(chan_ready, 1)
            act.wait_ge(gate_half_done, 1)
            act.wait_ge(pe_done, J_T1[6] + 1)
            nc.scalar.activation(tmp[:, 0, 0:HALF], slot_of(J_IN[1])[:, 0:HALF], ACT.Sigmoid)\
              .then_inc(sig_half_done, 1)
            act.wait_ge(pool_w_loaded, 16)
            act.wait_ge(normed, TT)
            nc.scalar.activation(pw_hi[:, :, :], pw_raw, ACT.Copy).then_inc(pw_done, 1)

            def gate_sigmoid(j):
                n = J_IN[2 * j + 1]
                act.wait_ge(pe_done, n + 1)
                if j >= 2:
                    act.wait_ge(u_done, j - 1)
                a = HALF if j == 0 else 0
                nc.scalar.activation(tmp[:, j % 2, a:SEQ], slot_of(n)[:, a:SEQ], ACT.Sigmoid).then_inc(sig_done, 1)

            def pool_tokens(g):
                n = J_IN[2 * CT + GROUPS - 1 - g]
                act.wait_ge(pe_done, n + 1)
                nc.scalar.activation(tokens[:, g, :], slot_of(n)[:, :], ACT.Copy).then_inc(tokens_ready, 1)

            def light_products(j, h, first=0, end=TAPS):
                if first == 0:
                    act.wait_ge(u_done, j + 1)
                    nc.scalar.activation(conv[:, h, j, :], u[:, j, h * HALF:(h + 1) * HALF], ACT.Identity,
                                         scale=chan[:, j, TAPS - 1:TAPS], bias=chan[:, j, BIAS:BIAS + 1])\
                      .then_inc(first_tap_done, 1)
                for s in range(max(first, 1), min(end, LIGHT[j, h])):
                    n = light_before[j, h] + s - 1
                    if n >= RING:
                        act.wait_ge(light_step, n - RING + 1)
                    a = max(h * HALF, s)
                    nc.scalar.activation(prod[:, n % RING, a - h * HALF:HALF], u[:, j, a - s:(h + 1) * HALF - s],
                                         ACT.Copy, scale=chan[:, j, TAPS - 1 - s:TAPS - s]).then_inc(product_done, 1)

            def ln_z(h):
                a = h * HT
                act.wait_ge(ln_step, LN_STEPS * h + 2 * HT)
                nc.scalar.activation(std[:, LN, a:a + HT], mean_var[:, a:a + HT, 1], ACT.Sqrt,
                                     bias=eps[:, 0:1]).then_inc(ln_std_done, 1)
                act.wait_ge(ln_step, LN_STEPS * (h + 1))
                for i in range(HT):
                    bank = slice((i % 2) * BANK, (i % 2 + 1) * BANK)
                    nc.scalar.activation(z_sb[:, i // 2, bank], slot_of(J_LN[h][i // 2])[:, bank], ACT.Identity,
                                         bias=shift[:, a + i:a + i + 1],
                                         scale=rstd[:, LN, a + i:a + i + 1]).then_inc(z_done, 1)

            def ln_silu(h):
                for j in range(CT):
                    n = J_BACK[h][j // 2]
                    y = slot_of(n)[:, (j % 2) * BANK:(j % 2 + 1) * BANK]
                    act.wait_ge(pe_done, n + 1)
                    nc.scalar.activation(y, y, ACT.Silu, scale=chan[:, j, LN_G:LN_G + 1],
                                         bias=chan[:, j, LN_B:LN_B + 1]).then_inc(silu_done, 1)
                    act.wait_ge(silu_done, h * CT + j + 1)
                    nc.scalar.activation(act_hi[:, j, h * HALF:(h + 1) * HALF], y,
                                         ACT.Copy).then_inc(act_hi_done, 1)

            unit_hi(2)
            gate_sigmoid(0)
            act.wait_ge(pw_done, 2)
            light_products(0, 1, 0, 9)
            unit_hi(3, J_IN[2])
            light_products(0, 1, 9)
            gate_sigmoid(1)
            unit_hi(4, J_IN[3])
            light_products(1, 0)
            gate_sigmoid(2)
            light_products(2, 0, 0, 8)
            unit_hi(5, J_IN[6])
            light_products(2, 0, 8)
            gate_sigmoid(3)
            light_products(3, 0)
            unit_hi(6, J_IN[7])
            pool_tokens(3)
            pool_tokens(2)
            unit_hi(7, J_IN[9])
            light_products(2, 1, 0, 5)
            pool_tokens(1)
            ln_z(0)
            light_products(2, 1, 5, 7)
            ln_silu(0)
            pool_tokens(0)

            def difference_hi(n):
                g = GROUPS - 1 - n
                act.wait_ge(d_step, 3 * (n + 1))
                nc.scalar.activation(act_hi[:, CT + g, :], tokens[:, g, :], ACT.Copy).then_inc(act_hi_done, 1)

            def pool_output(n):
                g = GROUPS - 1 - n
                act.wait_ge(pe_done, J_POOL[n] + 1)
                nc.scalar.activation(act_hi[:, CT + g, :], slot_of(J_POOL[n])[:, :], ACT.Copy,
                                     scale=chan[:, g, SCALE:SCALE + 1]).then_inc(act_hi_done, 1)

            difference_hi(0)
            light_products(2, 1, 7, 8)
            difference_hi(1)
            difference_hi(2)
            pool_output(0)
            pool_output(1)
            light_products(2, 1, 8, 10)
            difference_hi(3)
            unit_hi(8, J_IN[2 * CT + 3])
            light_products(2, 1, 10, 11)
            pool_output(2)
            act.wait_ge(act_lo_done, DONE["diff", GROUPS - 1])
            unit_hi(9)
            light_products(2, 1, 11, 13)
            pool_output(3)
            light_products(2, 1, 13)
            light_products(3, 1, 0, 8)

            def ffn_hi(kind, i, t, q, par, last_user=None):
                act.wait_ge(raw_loaded[par], raw_loads(q, par))
                if last_user is not None:
                    act.wait_ge(pe_done, last_user + 1)
                nc.scalar.activation(half_of(w_hi[ffn_slot(kind, i)][:, :], kind != "d", t),
                                     half_of(raw[:, par, :], kind != "d", t), ACT.Copy).then_inc(hi_done, 1)

            def t2_std(m):
                act.wait_ge(x1_done, m + 1)
                if m >= 2:
                    act.wait_ge(pe_done, J_T2[m - 2] + 1)
                norm_std(FFN, m)

            t2_std(0)
            light_products(3, 1, 8, 11)
            t2_std(1)
            light_products(3, 1, 11, 15)
            transposed_hi(J_T2[0], 0)
            light_products(3, 1, 15)
            t2_std(2)
            transposed_hi(J_T2[1], 1)
            ln_z(1)
            t2_std(3)
            ln_silu(1)
            transposed_hi(J_T2[2], 2)
            for m in range(HT, TT):
                t2_std(m)
                transposed_hi(J_T2[m - 1], m - 1)
                if m == TT - 2:
                    act.wait_ge(out_used, 1)
                    ffn_hi("g", 0, 0, U_FFN, 0)
                    act.wait_ge(out_used, 2)
                    ffn_hi("v", 0, 0, U_FFN + 1, 1)
            ffn_hi("g", 0, 1, U_FFN, 0)
            transposed_hi(J_T2[TT - 1], TT - 1)
            ffn_hi("v", 0, 1, U_FFN + 1, 1)

            def body(i, par, first=False, last=False):
                q = i * 3 + (U_FFN + 1)
                gq, vq, gpar, vpar = (q + 1, q + 2, par, 1 - par) if not first else (U_FFN + 2, U_FFN + 3, 0, 1)
                if not first:
                    before = i * BODY + (J_BODY - BODY - 1)
                    for t in range(2):
                        ffn_hi("d", i - 1, t, q, 1 - par, before)
                for t in range(2):
                    f = i * 2 + t
                    gate, value = up_job(i, 2 * t), up_job(i, 2 * t + 1)
                    c = fchan[:, f, :] if isinstance(i, int) else fchan[:, bass.ds(f, 1), :].squeeze(1)
                    act.wait_ge(pe_done, gate + 1)
                    if not first:
                        act.wait_ge(gv_lo_done, i * 2 + (t - 1))
                    nc.scalar.activation(tmp[:, t, :], slot[(F_SLOT + 2 * t) % 4][:, :], ACT.Identity,
                                         scale=c[:, FTAPS - 1:FTAPS], bias=c[:, FTAPS:FTAPS + 1])\
                      .then_inc(last_tap_done, 1)
                    if not last:
                        ffn_hi("g", i + 1, t, gq, gpar, gate)
                    act.wait_ge(gate_taps, i * 2 + (t + 1))
                    nc.scalar.activation(tmp[:, t, :], tmp[:, t, :], ACT.Silu).then_inc(gate_silu, 1)
                    if not last:
                        ffn_hi("v", i + 1, t, vq, vpar, value)
                    act.wait_ge(gated, i * 2 + (t + 1))
                    nc.scalar.activation(gv_hi[:, par, t, :], tmp[:, t, :], ACT.Copy).then_inc(gv_hi_done, 1)

            body(0, 0, first=True)
            with act.Fori(1, CHUNKS - 2, 2) as i:
                body(i, 1)
                body(i + 1, 0)
            body(CHUNKS - 2, 1)
            body(CHUNKS - 1, 0, last=True)
            for t in range(2):
                ffn_hi("d", CHUNKS - 1, t, U_FFN + 3 * CHUNKS - 1, 0, up_job(CHUNKS - 1, 2))
            act.wait_ge(gv_lo_done, FT)
            for m in range(TT):
                act.wait_ge(x2_done, m + 1)
                norm_std(FINAL, m)

        @block.vector
        def _(dve):
            def norm_apply(row, m, gains):
                n = row * TT + m + 1
                dve.wait_ge(std_done, n)
                nc.vector.reciprocal(rstd[:, row, m:m + 1], std[:, row, m:m + 1]).then_inc(rstd_done, 1)
                dve.wait_ge(rstd_done, n)
                dve.wait_ge(gain_loaded, 16 * gains)
                if row == FINAL:
                    if m >= 4:
                        dve.wait_ge(stored[m % 4], 16)
                    dst, done = raw[:, m % 4 // 2, (m % 2) * D:(m % 2 + 1) * D], out_ready
                else:
                    dst, done = tmp[:, m % 2, :], normed
                nc.vector.scalar_tensor_tensor(dst, x_sb[:, m, :], rstd[:, row, m:m + 1], gain[:, :],
                                               ALU.mult, ALU.mult).then_inc(done, 1)

            def transposed_lo(n, m, count):
                dve.wait_ge(act_hi_done, count)
                cols = slice(m * P, (m + 1) * P)
                nc.vector.tensor_tensor(act_lo[:, :, cols], slot_of(n)[:, :].rearrange("p (k n) -> p k n", k=KT),
                                        act_hi[:, :, cols].bitcast(F32), ALU.subtract).then_inc(act_lo_done, 1)

            def unit_lo(q):
                s, columns = W_SLOT[q], q < U_OUT
                for t in range(2):
                    dve.wait_ge(hi_done, 2 * q + t + 1)
                    nc.vector.tensor_tensor(half_of(w_lo[s][:, :], columns, t),
                                            half_of(raw[:, q % 2, :], columns, t),
                                            half_of(w_hi[s][:, :].bitcast(F32), columns, t),
                                            ALU.subtract).then_inc(lo_done, 1)

            for m in range(TT):
                norm_apply(IN, m, 1)
                if m >= 1:
                    transposed_lo(J_T1[m - 1], m - 1, DONE["t1", m - 1])
            transposed_lo(J_T1[TT - 1], TT - 1, DONE["t1", TT - 1])
            apart_sum = [z_sb[:, h, 0:HALF] for h in range(2)]
            taps_made = {}
            conv_count = [0]
            last_step = {}

            def one_tap(j, h):
                s = taps_made.get((j, h), LIGHT.get((j, h), 0))
                taps_made[j, h] = s + 1
                tap = chan[:, j, TAPS - 1 - s:TAPS - s]
                a, e = max(h * HALF, s), (h + 1) * HALF
                apart = j == APART
                dst = (apart_sum[h] if apart else conv[:, h, j, :])[:, a - h * HALF:HALF]
                if apart and s == LIGHT[j, h]:
                    if h == 1:
                        dve.wait_ge(pe_done, J_BACK[0][1] + 1)
                    op = nc.vector.tensor_scalar(dst, u[:, j, a - s:e - s], tap, None, ALU.mult)
                elif s == 0:
                    op = nc.vector.tensor_scalar(dst, u[:, j, a:e], tap, chan[:, j, BIAS:BIAS + 1],
                                                 ALU.mult, ALU.add)
                else:
                    if s == LIGHT.get((j, h)):
                        dve.wait_ge(light_step, light_before[j, h] + s - 1)
                    else:
                        dve.wait_ge(conv_step, last_step[j, h])
                    op = nc.vector.scalar_tensor_tensor(dst, u[:, j, a - s:e - s], tap, dst, ALU.mult, ALU.add)
                if s == TAPS - 1 and not apart:
                    op.then_inc(conv_done[h], 1)
                else:
                    op.then_inc(conv_step, 1)
                    conv_count[0] += 1
                    last_step[j, h] = conv_count[0]

            def add_apart(h):
                j, s = APART, LIGHT[APART, h]
                a = s if h == 0 else 0
                dve.wait_ge(light_step, light_before[j, h] + s - 1)
                dve.wait_ge(conv_step, last_step[j, h])
                nc.vector.tensor_tensor(conv[:, h, j, a:HALF], conv[:, h, j, a:HALF], apart_sum[h][:, a:HALF],
                                        ALU.add).then_inc(conv_done[h], 1)

            def conv_taps(*runs):
                for n in range(max(r[2] for r in runs)):
                    for j, h, count in runs:
                        if n < count:
                            one_tap(j, h)

            def make_u(j, half=None):
                dve.wait_ge(sig_half_done if half == 0 else sig_done, j + 1)
                a, e = (0, SEQ) if half is None else (half * HALF, (half + 1) * HALF)
                nc.vector.tensor_tensor(u[:, j, a:e], slot_of(J_IN[2 * j])[:, a:e], tmp[:, j % 2, a:e],
                                        ALU.mult).then_inc(u_half_done if half == 0 else u_done, 1)

            def pool_difference(g):
                n = GROUPS - 1 - g
                w, sums = WINDOWS[g], tmp[:, g % 2, :]
                dve.wait_ge(window_step, WINDOW_STEPS[g])
                dve.wait_ge(small_ready, 1 + WINDOWS[-1])
                if n:
                    dve.wait_ge(d_step, 3 * n)
                nc.vector.tensor_tensor(edge[:, 0:w - 1], sums[:, 0:w - 1], inv_count[:, 0:w - 1],
                                        ALU.mult).then_inc(d_step, 1)
                nc.vector.scalar_tensor_tensor(tokens[:, g, w - 1:SEQ], sums[:, w - 1:SEQ], 1.0 / w,
                                               tokens[:, g, w - 1:SEQ], ALU.mult, ALU.subtract)\
                  .then_inc(d_step, 1)
                dve.wait_ge(d_step, 3 * n + 1)
                nc.vector.tensor_tensor(tokens[:, g, 0:w - 1], edge[:, 0:w - 1], tokens[:, g, 0:w - 1],
                                        ALU.subtract).then_inc(d_step, 1)

            def ln_stats(h):
                a, base = h * HT, LN_STEPS * h
                for i in range(HT):
                    n = J_LN[h][i // 2]
                    dve.wait_ge(pe_done, n + 1)
                    nc.vector.bn_stats(bn[:, a + i, :], slot_of(n)[:, (i % 2) * BANK:(i % 2 + 1) * BANK])\
                      .then_inc(ln_step, 1)
                for i in range(HT):
                    dve.wait_ge(ln_step, base + i + 1)
                    nc.vector.bn_aggr(mean_var[:, a + i, :], bn[:, a + i, :]).then_inc(ln_step, 1)
                if h == 0:
                    pool_difference(3)
                dve.wait_ge(ln_std_done, h + 1)
                nc.vector.reciprocal(rstd[:, LN, a:a + HT], std[:, LN, a:a + HT]).then_inc(ln_step, 1)
                dve.wait_ge(ln_step, base + 2 * HT + 1)
                nc.vector.scalar_tensor_tensor(shift[:, a:a + HT], mean_var[:, a:a + HT, 0], -1.0,
                                               rstd[:, LN, a:a + HT], ALU.mult, ALU.mult).then_inc(ln_step, 1)

            def ya_lo(h, first=0, end=CT):
                for j in range(first, end):
                    cols = slice(h * HALF, (h + 1) * HALF)
                    dve.wait_ge(act_hi_done, DONE["ya", h, j])
                    nc.vector.tensor_tensor(act_lo[:, j, cols],
                                            slot_of(J_BACK[h][j // 2])[:, (j % 2) * BANK:(j % 2 + 1) * BANK],
                                            act_hi[:, j, cols].bitcast(F32), ALU.subtract)\
                      .then_inc(act_lo_done, 1)

            def x1(m):
                dve.wait_ge(pe_done, J_OUT[m] + 1)
                if m >= HT:
                    dve.wait_ge(x_loaded[m], 32)
                nc.vector.tensor_tensor(x_sb[:, m, :], x_sb[:, m, :], slot_of(J_OUT[m])[:, :],
                                        ALU.add).then_inc(x1_done, 1)

            def t2_lo(m):
                transposed_lo(J_T2[m], m, DONE["t2", m])

            def difference_lo(n):
                g = GROUPS - 1 - n
                dve.wait_ge(act_hi_done, DONE["diff", n])
                nc.vector.tensor_tensor(act_lo[:, CT + g, :], tokens[:, g, :], act_hi[:, CT + g, :].bitcast(F32),
                                        ALU.subtract).then_inc(act_lo_done, 1)

            def yb_lo(n):
                g = GROUPS - 1 - n
                dve.wait_ge(act_hi_done, DONE["yb", n])
                nc.vector.scalar_tensor_tensor(act_lo[:, CT + g, :], slot_of(J_POOL[n])[:, :],
                                               chan[:, g, SCALE:SCALE + 1], act_hi[:, CT + g, :].bitcast(F32),
                                               ALU.mult, ALU.subtract).then_inc(act_lo_done, 1)

            dve.wait_ge(normed, TT)
            dve.wait_ge(chan_ready, 2)
            make_u(0, 0)
            dve.wait_ge(u_half_done, 1)
            conv_taps((0, 0, 11))
            conv_taps((0, 0, 2))
            make_u(0, 1)
            conv_taps((0, 0, 16))
            unit_lo(3)
            conv_taps((0, 0, 2))
            make_u(1)
            unit_lo(4)
            dve.wait_ge(u_done, 2)
            conv_taps((1, 1, 10), (0, 1, 14))
            make_u(2)
            dve.wait_ge(u_done, 3)
            conv_taps((1, 1, 4), (1, 0, 16))
            unit_lo(5)
            conv_taps((1, 1, 4))
            make_u(3)
            dve.wait_ge(u_done, 4)
            conv_taps((2, 0, 15))
            conv_taps((3, 0, 16))
            add_apart(0)
            unit_lo(6)
            conv_taps((1, 1, 3))
            ln_stats(0)
            unit_lo(7)
            conv_taps((1, 1, 5))
            ya_lo(0, 0, 2)
            pool_difference(2)
            ya_lo(0, 2)
            difference_lo(0)
            difference_lo(1)
            pool_difference(1)
            difference_lo(2)
            yb_lo(0)
            pool_difference(0)
            yb_lo(1)
            difference_lo(3)
            unit_lo(8)
            yb_lo(2)
            unit_lo(9)
            conv_taps((1, 1, 1))
            yb_lo(3)
            conv_taps((1, 1, 4), (3, 1, 4))
            conv_taps((2, 1, 4))
            x1(0)
            conv_taps((2, 1, 2), (3, 1, 2))
            norm_apply(FFN, 0, 2)
            x1(1)
            conv_taps((2, 1, 2), (3, 1, 2))
            norm_apply(FFN, 1, 2)
            conv_taps((2, 1, 6), (3, 1, 6))
            t2_lo(0)
            add_apart(1)
            x1(2)
            norm_apply(FFN, 2, 2)
            t2_lo(1)
            ln_stats(1)
            x1(3)
            norm_apply(FFN, 3, 2)
            ya_lo(1)
            x1(4)
            t2_lo(2)
            norm_apply(FFN, 4, 2)
            t2_lo(3)

            def ffn_lo(kind, i, t, par):
                s = ffn_slot(kind, i)
                dve.wait_ge(hi_done, ffn_half(kind, i, t) + HI0)
                nc.vector.tensor_tensor(half_of(w_lo[s][:, :], kind != "d", t),
                                        half_of(raw[:, par, :], kind != "d", t),
                                        half_of(w_hi[s][:, :].bitcast(F32), kind != "d", t),
                                        ALU.subtract).then_inc(lo_done, 1)

            for m in range(HT + 1, TT):
                x1(m)
                norm_apply(FFN, m, 2)
                t2_lo(m - 1)
                if m == TT - 2:
                    ffn_lo("g", 0, 0, 0)
                    ffn_lo("v", 0, 0, 1)
            ffn_lo("g", 0, 1, 0)
            t2_lo(TT - 1)
            ffn_lo("v", 0, 1, 1)

            def gate(i, t):
                f = i * 2 + t
                c = fchan[:, f, :] if isinstance(i, int) else fchan[:, bass.ds(f, 1), :].squeeze(1)
                ps = slot[(F_SLOT + 2 * t) % 4]
                dve.wait_ge(last_tap_done, i * 2 + (t + 1))
                for s in (1, 2):
                    if s == 2:
                        dve.wait_ge(gate_one, i * 2 + (t + 1))
                    nc.vector.scalar_tensor_tensor(tmp[:, t, s:SEQ], ps[:, 0:SEQ - s],
                                                   c[:, FTAPS - 1 - s:FTAPS - s], tmp[:, t, s:SEQ],
                                                   ALU.mult, ALU.add).then_inc(gate_one if s == 1 else gate_taps, 1)

            def gate_times_value(i, t):
                dve.wait_ge(gate_silu, i * 2 + (t + 1))
                dve.wait_ge(pe_done, up_job(i, 2 * t + 1) + 1)
                nc.vector.tensor_tensor(tmp[:, t, :], tmp[:, t, :], slot[(F_SLOT + 2 * t + 1) % 4][:, :],
                                        ALU.mult).then_inc(gated, 1)

            def gv_low(i, t, par):
                dve.wait_ge(gv_hi_done, i * 2 + (t + 1))
                nc.vector.tensor_tensor(gv_lo[:, par, t, :], tmp[:, t, :], gv_hi[:, par, t, :].bitcast(F32),
                                        ALU.subtract).then_inc(gv_lo_done, 1)

            def add_down(i, m):
                dve.wait_ge(pe_done, down_job(i, m) + 1)
                if isinstance(i, int) and i == 0:
                    dve.wait_ge(normed, 2 * TT)
                else:
                    dve.wait_ge(x_added, i * TT + (m - TT + 1))
                last = isinstance(i, int) and i == CHUNKS - 1
                nc.vector.tensor_tensor(x_sb[:, m, :], x_sb[:, m, :], slot[(F_SLOT + m) % 4][:, :],
                                        ALU.add).then_inc(x2_done if last else x_added, 1)

            def body(i, par, down=True, last=False):
                gpar, vpar = (par, 1 - par) if down else (0, 1)
                if down:
                    ffn_lo("d", i - 1, 0, 1 - par)
                    ffn_lo("d", i - 1, 1, 1 - par)
                gate(i, 0)
                if not last:
                    ffn_lo("g", i + 1, 0, gpar)
                gate_times_value(i, 0)
                if not last:
                    ffn_lo("v", i + 1, 0, vpar)
                gv_low(i, 0, par)
                gate(i, 1)
                if not last:
                    ffn_lo("g", i + 1, 1, gpar)
                gate_times_value(i, 1)
                if not last:
                    ffn_lo("v", i + 1, 1, vpar)
                if down:
                    add_down(i - 1, 0)
                gv_low(i, 1, par)
                if last:
                    for t in range(2):
                        ffn_lo("d", i, t, 0)
                if down:
                    for m in range(1, TT):
                        add_down(i - 1, m)

            body(0, 0, down=False)
            body(1, 1)
            body(2, 0)
            with dve.Fori(3, CHUNKS - 2, 2) as i:
                body(i, 1)
                body(i + 1, 0)
            body(CHUNKS - 2, 1)
            body(CHUNKS - 1, 0, last=True)
            dve.wait_ge(lo_done, LO0 + ffn_half("d", CHUNKS - 1, 1))
            for m in range(TT):
                add_down(CHUNKS - 1, m)
                if m >= 1:
                    norm_apply(FINAL, m - 1, 3)
            norm_apply(FINAL, TT - 1, 3)

        @block.tensor
        def _(pe):
            last_in = {}

            def slot_read(n):
                if SLOT[n] in last_in:
                    pe.wait_ge(*read[last_in[SLOT[n]]])
                last_in[SLOT[n]] = n

            def three_passes(out_ap, st, mv, first, last):
                for s, v in ((0, 0), (0, 1), (1, 0)):
                    mm = nc.tensor.matmul(out_ap, st[s], mv[v], start=first and s == v == 0,
                                          stop=last and s == 1)
                return mm

            act = (act_hi, act_lo)
            bank = [slice(0, BANK), slice(BANK, 2 * BANK)]

            def constants():
                pe.wait_ge(consts_loaded, 16 * 7)
                slot_read(J_CONST)
                ps = slot_of(J_CONST)
                for c in range(CT):
                    nc.tensor.transpose(ps[:, c * ROWS:(c + 1) * ROWS], raw_rows[0:ROWS, c * P:(c + 1) * P],
                                        ident[0:ROWS, 0:ROWS])
                R = FTAPS + 1
                for c in range(FT):
                    mm = nc.tensor.transpose(ps[:, BANK + c * R:BANK + (c + 1) * R],
                                             raw_frows[0:R, c * P:(c + 1) * P], ident[0:R, 0:R])
                mm.then_inc(pe_done, 1)

            def transpose_tile(n, m, count):
                slot_read(n)
                pe.wait_ge(normed, count)
                for k in range(KT):
                    mm = nc.tensor.transpose(slot_of(n)[:, k * P:(k + 1) * P], tmp[:, m % 2, k * P:(k + 1) * P],
                                             ident[:, :])
                mm.then_inc(pe_done, 1)

            pe.wait_ge(ident_ready, 2)
            for m in range(HT + 1):
                transpose_tile(J_T1[m], m, m + 1)

            def column_part(ps, s, t, h):
                w = [whole(b[s][:, :], True)[:, :, t * P:(t + 1) * P] for b in (w_hi, w_lo)]
                for k in range(KT):
                    mm = three_passes(ps[:, bank[h]], [b[:, k, :] for b in w],
                                      [a[:, k, bank[h]] for a in act], k == 0, k == KT - 1)
                return mm

            def column_tile(ps, s, t):
                column_part(ps, s, t, 0)
                column_part(ps, s, t, 1).then_inc(pe_done, 1)

            order = [(2 * (j // 2) + b, j % 2) for j in range(CT) for b in range(2)] + [(4, 1), (4, 0), (5, 1), (5, 0)]

            def in_projection(n):
                q, t = order[n]
                slot_read(J_IN[n])
                if q < POOL_UNITS:
                    pe.wait_ge(lo_pool_done, half_count(q, t))
                else:
                    pe.wait_ge(lo_done, 2 * (q - POOL_UNITS) + t + 1)
                column_tile(slot_of(J_IN[n]), W_SLOT[q], t)

            for n in range(2):
                slot_read(J_IN[n])
                pe.wait_ge(lo_pool_done, half_count(n, 0))
                pe.wait_ge(act_lo_done, DONE["t1", HT - 1])
                mm = column_part(slot_of(J_IN[n]), W_SLOT[n], 0, 0)
                if n == 1:
                    mm.then_inc(gate_half_done, 1)
                for m in ((5, 6), (7,))[n]:
                    transpose_tile(J_T1[m], m, m + 1)
            constants()
            pe.wait_ge(act_lo_done, DONE["t1", TT - 1])
            for n in range(2):
                column_part(slot_of(J_IN[n]), W_SLOT[n], 0, 1).then_inc(pe_done, 1)
            for n in range(2):
                pe.wait_ge(lo_pool_done, half_count(n, 1))
                slot_read(J_IN[2 + n])
                column_tile(slot_of(J_IN[2 + n]), W_SLOT[n], 1)

            def ln_to_tokens(h):
                pe.wait_ge(conv_done[h], CT)
                for b in range(2):
                    n = J_LN[h][b]
                    slot_read(n)
                    for i in range(2):
                        for j in range(CT):
                            cols = slice((2 * b + i) * P, (2 * b + i + 1) * P)
                            mm = nc.tensor.transpose(slot_of(n)[:, i * BANK + j * P:i * BANK + (j + 1) * P],
                                                     conv[:, h, j, cols], ident[:, :])
                    mm.then_inc(pe_done, 1)

            def ln_back(h):
                pe.wait_ge(z_done, HT * (h + 1))
                for b in range(2):
                    n = J_BACK[h][b]
                    slot_read(n)
                    for jj in range(2):
                        for i in range(HT):
                            at = (i % 2) * BANK + (2 * b + jj) * P
                            mm = nc.tensor.transpose(slot_of(n)[:, jj * BANK + i * P:jj * BANK + (i + 1) * P],
                                                     z_sb[:, i // 2, at:at + P], ident[:, :])
                    mm.then_inc(pe_done, 1)

            def out_units(m, rs, first=False, last=False):
                n = J_OUT[m]
                if first:
                    slot_read(n)
                cols = slice(m * P, (m + 1) * P)
                for r in rs:
                    q, k0 = U_OUT + r, OUT_ROWS[r]
                    made = ("ya", m // HT, CT - 1) if r < 2 else ("yb", 2 * r - 3)
                    pe.wait_ge(act_lo_done, DONE[made])
                    pe.wait_ge(lo_done, 2 * (q - POOL_UNITS) + 2)
                    for kk in range(2):
                        for h in range(2):
                            mm = three_passes(slot_of(n)[:, bank[h]], [a[:, k0 + kk, cols] for a in act],
                                              [whole(b[W_SLOT[q]][:, :], False)[:, kk, bank[h]] for b in (w_hi, w_lo)],
                                              first and r == rs[0] and kk == 0, last and r == rs[-1] and kk == 1)
                    if m == TT - 1 and r < 2:
                        mm.then_inc(out_used, 1)
                if last:
                    mm.then_inc(pe_done, 1)

            def out_projection(m):
                out_units(m, (0, 1, 2, 3), True, True)

            def t2(m):
                transpose_tile(J_T2[m], m, TT + m + 1)

            for n in range(4, 2 * CT + 3):
                in_projection(n)
            ln_to_tokens(0)
            q, t = order[-1]
            slot_read(J_IN[-1])
            pe.wait_ge(lo_done, 2 * (q - POOL_UNITS) + t + 1)
            column_part(slot_of(J_IN[-1]), W_SLOT[q], t, 0)
            ln_back(0)
            column_part(slot_of(J_IN[-1]), W_SLOT[q], t, 1).then_inc(pe_done, 1)

            def pool_product(n):
                g = GROUPS - 1 - n
                slot_read(J_POOL[n])
                pe.wait_ge(act_lo_done, DONE["diff", n])
                for h in range(2):
                    mm = three_passes(slot_of(J_POOL[n])[:, bank[h]], (pw_hi[:, g, :], pw_lo[:, g, :]),
                                      [a[:, CT + g, bank[h]] for a in act], True, True)
                mm.then_inc(pe_done, 1)

            out_units(0, (0, 1), first=True)
            pe.wait_ge(pw_done, 2)
            pool_product(0)
            pool_product(1)
            out_units(1, (0,), first=True)
            pool_product(2)
            out_units(1, (1,))
            pool_product(3)
            out_units(0, (2,))
            out_units(1, (2,))
            out_units(0, (3,), last=True)
            out_units(1, (3,), last=True)
            out_projection(2)
            t2(0)
            out_units(3, (0, 1), first=True)
            t2(1)
            out_units(3, (2,))
            ln_to_tokens(1)
            out_units(3, (3,), last=True)
            out_units(4, (2, 3), first=True)
            ln_back(1)
            out_units(5, (2, 3), first=True)
            out_units(4, (0, 1), last=True)
            t2(2)
            t2(3)
            out_units(5, (0, 1), last=True)
            t2(4)
            out_projection(6)
            t2(5)
            out_projection(7)

            def up(i, t, kind):
                r = 2 * t + (kind == "v")
                if isinstance(i, int) and i == 1:
                    pe.wait_ge(gate_taps if kind == "g" else gated, t + 1)
                else:
                    pe.wait_ge(x_added, i * TT + (r + UPS - 2 * TT + 1))
                pe.wait_ge(lo_done, ffn_half(kind, i, t) + LO0)
                column_tile(slot[(F_SLOT + r) % 4], ffn_slot(kind, i), t)

            def down(i, par):
                last = isinstance(i, int) and i == CHUNKS - 1
                for m in range(TT):
                    if m < UPS:
                        if last:
                            pe.wait_ge(x_added, i * TT + (m - UPS + 1))
                        else:
                            pe.wait_ge(gated if m % 2 else gate_taps, i * 2 + (2 + m // 2 + 1))
                    else:
                        pe.wait_ge(x2_done if last else x_added, (0 if last else i * TT) + (m - UPS + 1))
                    if m == 0:
                        pe.wait_ge(lo_done, ffn_half("d", i, 1) + LO0)
                        pe.wait_ge(gv_lo_done, i * 2 + 2)
                    cols = slice(m * P, (m + 1) * P)
                    for kk in range(2):
                        for h in range(2):
                            mm = three_passes(slot[(F_SLOT + m) % 4][:, bank[h]],
                                              [b[:, par, kk, cols] for b in (gv_hi, gv_lo)],
                                              [whole(b[ffn_slot("d", i)][:, :], False)[:, kk, bank[h]]
                                               for b in (w_hi, w_lo)], kk == 0, kk == 1)
                    mm.then_inc(pe_done, 1)

            def body(i, par):
                for t in range(2):
                    up(i, t, "g")
                    up(i, t, "v")
                down(i - 1, 1 - par)

            pe.wait_ge(act_lo_done, DONE["t2", HT - 1])
            for r, kind in enumerate("gv"):
                slot_read(J_FFN + r)
                pe.wait_ge(lo_done, LO0 + ffn_half(kind, 0, 0))
                column_part(slot_of(J_FFN + r), ffn_slot(kind, 0), 0, 0)
                t2(TT - 2 + r)
            slot_read(J_FFN + 2)
            pe.wait_ge(lo_done, LO0 + ffn_half("g", 0, 1))
            column_part(slot_of(J_FFN + 2), ffn_slot("g", 0), 1, 0)
            pe.wait_ge(act_lo_done, DONE["t2", TT - 1])
            for r, kind in enumerate("gvg"):
                column_part(slot_of(J_FFN + r), ffn_slot(kind, 0), r // 2, 1).then_inc(pe_done, 1)
            slot_read(J_FFN + 3)
            pe.wait_ge(lo_done, LO0 + ffn_half("v", 0, 1))
            column_tile(slot_of(J_FFN + 3), ffn_slot("v", 0), 1)
            body(1, 1)
            body(2, 0)
            with pe.Fori(3, CHUNKS - 2, 2) as i:
                body(i, 1)
                body(i + 1, 0)
            body(CHUNKS - 2, 1)
            body(CHUNKS - 1, 0)
            down(CHUNKS - 1, 0)


_INS = ["x", "norm_mix_g", "w_in", "conv_a_w", "conv_a_b", "ln_a_g", "ln_a_b", "pool_w", "pool_scale",
        "w_out", "norm_ffn_g", "w_up", "conv_f_w", "conv_f_b", "w_down", "norm_final_g"]


def kernel(**inputs):
    import numpy as np
    import concourse.bacc as bacc
    from concourse.bass_utils import run_bass_kernel_spmd

    nc = bacc.Bacc("TRN2", target_bir_lowering=False, num_devices=1,
                   dynamic_dma_scratch_size=1024)
    arrays, args = {}, []
    for name in _INS:
        a = np.ascontiguousarray(inputs[name])
        arrays[f"in_{name}"] = a
        args.append(nc.dram_tensor(f"in_{name}", a.shape, mybir.dt.from_np(a.dtype), kind="ExternalInput").ap())
    out = nc.dram_tensor("out_0", inputs["x"].shape, F32, kind="ExternalOutput").ap()
    hybrid_block(nc, *args, out)
    result = run_bass_kernel_spmd(nc, [arrays], core_ids=[0])
    return result.results[0]["out_0"]
```
